# Optimizing a Trainium2 kernel written in Bass

```python
import jax, jax.numpy as jnp
from jax import lax
import numpy as np
import math

D_MODEL = 1024
BATCH = 1
SEQ = 512
DEPTH = 1

GRID_W = 64
N_Q_HEADS = 16
N_KV_HEADS = 4
HEAD_DIM = 64
ROPE_THETA = 10000.0
Q_BLOCK = 128
SSD_EXPAND = 2
D_INNER = SSD_EXPAND * D_MODEL
SSD_HEAD_DIM = 64
N_SSD_HEADS = D_INNER // SSD_HEAD_DIM
N_SSD_GROUPS = 4
D_STATE = 128
D_CONV = 5
CHUNK = 128
D_FF = 4 * D_MODEL
EPS = 1e-6

ATTN_Q_DIM = N_Q_HEADS * HEAD_DIM
ATTN_KV_DIM = N_KV_HEADS * HEAD_DIM
CONV_DIM = D_INNER + 2 * N_SSD_GROUPS * D_STATE
D_IN_PROJ = ATTN_Q_DIM + 2 * ATTN_KV_DIM + CONV_DIM + D_INNER + 2 * N_SSD_HEADS + 2 * D_MODEL


def rms_norm(x, w):
    xf = x.astype(jnp.float32)
    xf = xf * lax.rsqrt(jnp.mean(xf * xf, axis=-1, keepdims=True) + EPS)
    return xf.astype(x.dtype) * w

def rotate(u, cos, sin):
    f = u.shape[-1] // 2
    u1, u2 = u[..., :f], u[..., f:]
    cos = cos[None, :, None, :]
    sin = sin[None, :, None, :]
    return jnp.concatenate([u1 * cos - u2 * sin, u2 * cos + u1 * sin], axis=-1)

def axial_rope(t, cos_r, sin_r, cos_c, sin_c):
    half = t.shape[-1] // 2
    out = jnp.concatenate([rotate(t[..., :half], cos_r, sin_r),
                           rotate(t[..., half:], cos_c, sin_c)], axis=-1)
    return out.astype(t.dtype)

def block_attention(q, k, v):
    b, s, hq, dh = q.shape
    hkv = k.shape[2]
    rep = hq // hkv
    nb = s // Q_BLOCK
    qb = q.reshape(b, nb, Q_BLOCK, hkv, rep, dh).transpose(1, 0, 2, 3, 4, 5)
    scale = dh ** -0.5

    def one_block(qi):
        sc = jnp.einsum("bqgrd,bkgd->bgrqk", qi, k).astype(jnp.float32) * scale
        p = jax.nn.softmax(sc, axis=-1).astype(v.dtype)
        return jnp.einsum("bgrqk,bkgd->bqgrd", p, v)

    out = lax.map(one_block, qb)
    return out.transpose(1, 0, 2, 3, 4, 5).reshape(b, s, hq * dh)

def segsum(a):
    t = a.shape[-1]
    cs = jnp.cumsum(a, axis=-1)
    diff = cs[..., :, None] - cs[..., None, :]
    mask = jnp.tril(jnp.ones((t, t), dtype=bool))
    return jnp.where(mask, diff, -jnp.inf)

def ssd_chunked(xdt, a, bm, cm):
    b, s, h, p = xdt.shape
    g, n = bm.shape[2], bm.shape[3]
    r = h // g
    nc = s // CHUNK
    X = xdt.astype(jnp.float32).reshape(b, nc, CHUNK, g, r, p)
    A = a.reshape(b, nc, CHUNK, g, r).transpose(0, 3, 4, 1, 2)
    Bc = bm.astype(jnp.float32).reshape(b, nc, CHUNK, g, n)
    Cc = cm.astype(jnp.float32).reshape(b, nc, CHUNK, g, n)
    A_cs = jnp.cumsum(A, axis=-1)
    CB = jnp.einsum("bclgn,bcsgn->bgcls", Cc, Bc)
    M = CB[:, :, None] * jnp.exp(segsum(A))
    y_diag = jnp.einsum("bgrcls,bcsgrp->bclgrp", M, X)
    decay_states = jnp.exp(A_cs[..., -1:] - A_cs)
    states = jnp.einsum("bclgn,bgrcl,bclgrp->cbgrpn", Bc, decay_states, X)
    chunk_decay = jnp.moveaxis(jnp.exp(A_cs[..., -1]), -1, 0)

    def step(hs, inp):
        st, dec = inp
        return dec[..., None, None] * hs + st, hs

    h0 = jnp.zeros(states.shape[1:], jnp.float32)
    _, prev = lax.scan(step, h0, (states, chunk_decay))
    y_off = jnp.einsum("bclgn,cbgrpn,bgrcl->bclgrp", Cc, prev, jnp.exp(A_cs))
    return (y_diag + y_off).reshape(b, s, h, p)

def depthwise_conv_centred(u, w, bias):
    pad = (w.shape[0] - 1) // 2
    out = lax.conv_general_dilated(u, w[:, None, :].astype(u.dtype), window_strides=(1,),
                                   padding=[(pad, pad)], dimension_numbers=("NWC", "WIO", "NWC"),
                                   feature_group_count=u.shape[-1])
    return out + bias

def ssd_mixer(xBC, z, dt_raw, conv_w, conv_b, A_log, dt_bias, ssd_D, ssd_norm_w):
    b, s, _ = xBC.shape
    xBC = jax.nn.silu(depthwise_conv_centred(xBC, conv_w, conv_b))
    gn = N_SSD_GROUPS * D_STATE
    xs = xBC[..., :D_INNER].reshape(b, s, N_SSD_HEADS, SSD_HEAD_DIM)
    bm = xBC[..., D_INNER:D_INNER + gn].reshape(b, s, N_SSD_GROUPS, D_STATE)
    cm = xBC[..., D_INNER + gn:].reshape(b, s, N_SSD_GROUPS, D_STATE)
    dt = jax.nn.softplus(dt_raw.astype(jnp.float32).reshape(b, s, 2, N_SSD_HEADS)
                         + dt_bias.astype(jnp.float32))
    A = -jnp.exp(A_log.astype(jnp.float32))
    dt_f, dt_b = dt[:, :, 0], dt[:, :, 1]
    xf = xs.astype(jnp.float32)
    y_fwd = ssd_chunked(xf * dt_f[..., None], dt_f * A[0], bm, cm)
    flip = lambda t: jnp.flip(t, axis=1)
    y_bwd = flip(ssd_chunked(flip(xf * dt_b[..., None]), flip(dt_b * A[1]), flip(bm), flip(cm)))
    y = y_fwd + y_bwd + ssd_D.astype(jnp.float32)[:, None] * xf
    y = y.reshape(b, s, D_INNER).astype(xBC.dtype)
    return rms_norm(y * jax.nn.silu(z), ssd_norm_w)

def first_inputs(seed: int = 0) -> dict:
    key = jax.random.key(seed)
    ks = jax.random.split(key, 20)
    f32 = jnp.float32
    L = DEPTH
    nrm = lambda k, shape, s: jax.random.normal(k, shape, f32) * s
    x = jax.random.normal(ks[0], (BATCH, SEQ, D_MODEL), f32)
    c = jax.random.normal(ks[1], (BATCH, D_MODEL), f32)
    w_ada = nrm(ks[2], (L, D_MODEL, 6 * D_MODEL), 0.5 * D_MODEL ** -0.5)
    b_ada = nrm(ks[3], (L, 6 * D_MODEL), 0.02)
    norm1_w = 1.0 + nrm(ks[4], (L, D_MODEL), 0.02)
    norm2_w = 1.0 + nrm(ks[5], (L, D_MODEL), 0.02)
    w_in = nrm(ks[6], (L, D_MODEL, D_IN_PROJ), D_MODEL ** -0.5)
    q_norm_w = 1.0 + nrm(ks[7], (L, HEAD_DIM), 0.02)
    k_norm_w = 1.0 + nrm(ks[8], (L, HEAD_DIM), 0.02)
    conv_w = nrm(ks[9], (L, D_CONV, CONV_DIM), D_CONV ** -0.5)
    conv_b = nrm(ks[10], (L, CONV_DIM), 0.02)
    A_log = jnp.log(jax.random.uniform(ks[11], (L, 2, N_SSD_HEADS), f32, 1.0, 16.0))
    dt0 = jnp.exp(jax.random.uniform(ks[12], (L, 2, N_SSD_HEADS), f32, np.log(1e-3), np.log(1e-1)))
    dt_bias = dt0 + jnp.log(-jnp.expm1(-dt0))
    ssd_D = 1.0 + nrm(ks[13], (L, N_SSD_HEADS), 0.02)
    ssd_norm_w = 1.0 + nrm(ks[14], (L, D_INNER), 0.02)
    w_attn_out = nrm(ks[15], (L, ATTN_Q_DIM, D_MODEL), ATTN_Q_DIM ** -0.5)
    w_ssd_out = nrm(ks[16], (L, D_INNER, D_MODEL), D_INNER ** -0.5)
    w_o = nrm(ks[17], (L, D_MODEL, D_MODEL), D_MODEL ** -0.5)
    w_mlp1 = nrm(ks[18], (L, D_MODEL, D_FF), D_MODEL ** -0.5)
    w_mlp2 = nrm(ks[19], (L, D_FF, D_MODEL), D_FF ** -0.5)
    return {"x": x, "c": c, "w_ada": w_ada, "b_ada": b_ada, "norm1_w": norm1_w, "norm2_w": norm2_w,
            "w_in": w_in, "q_norm_w": q_norm_w, "k_norm_w": k_norm_w, "conv_w": conv_w, "conv_b": conv_b,
            "A_log": A_log, "dt_bias": dt_bias, "ssd_D": ssd_D, "ssd_norm_w": ssd_norm_w,
            "w_attn_out": w_attn_out, "w_ssd_out": w_ssd_out, "w_o": w_o,
            "w_mlp1": w_mlp1, "w_mlp2": w_mlp2}

def first_block(x, c, w_ada, b_ada, norm1_w, norm2_w, w_in, q_norm_w, k_norm_w, conv_w, conv_b,
              A_log, dt_bias, ssd_D, ssd_norm_w, w_attn_out, w_ssd_out, w_o, w_mlp1, w_mlp2):
    b, s, d = x.shape
    rows = s // GRID_W
    pos_row = jnp.repeat(jnp.arange(rows, dtype=jnp.int32), GRID_W).astype(jnp.float32)
    pos_col = jnp.tile(jnp.arange(GRID_W, dtype=jnp.int32), rows).astype(jnp.float32)
    axis_dim = HEAD_DIM // 2
    inv_freq = ROPE_THETA ** (-jnp.arange(0, axis_dim, 2, dtype=jnp.float32) / axis_dim)
    ang_r = pos_row[:, None] * inv_freq[None, :]
    ang_c = pos_col[:, None] * inv_freq[None, :]
    cos_r, sin_r = jnp.cos(ang_r), jnp.sin(ang_r)
    cos_c, sin_c = jnp.cos(ang_c), jnp.sin(ang_c)

    sizes = [ATTN_Q_DIM, ATTN_KV_DIM, ATTN_KV_DIM, CONV_DIM, D_INNER, 2 * N_SSD_HEADS, 2 * D_MODEL]
    offsets = []
    acc = 0
    for sz in sizes[:-1]:
        acc += sz
        offsets.append(acc)

    for l in range(DEPTH):
        mod = jax.nn.silu(c) @ w_ada[l] + b_ada[l]
        shift1, scale1, gate1, shift2, scale2, gate2 = [m[:, None, :] for m in jnp.split(mod, 6, axis=-1)]

        h = rms_norm(x, norm1_w[l]) * (1.0 + scale1) + shift1
        proj = h @ w_in[l]
        q, k, v, xBC, z, dt_raw, gates = jnp.split(proj, offsets, axis=-1)

        q = rms_norm(q.reshape(b, s, N_Q_HEADS, HEAD_DIM), q_norm_w[l])
        k = rms_norm(k.reshape(b, s, N_KV_HEADS, HEAD_DIM), k_norm_w[l])
        v = v.reshape(b, s, N_KV_HEADS, HEAD_DIM)
        q = axial_rope(q, cos_r, sin_r, cos_c, sin_c)
        k = axial_rope(k, cos_r, sin_r, cos_c, sin_c)
        attn = block_attention(q, k, v)

        ssd = ssd_mixer(xBC, z, dt_raw, conv_w[l], conv_b[l], A_log[l], dt_bias[l], ssd_D[l], ssd_norm_w[l])

        g_attn = jax.nn.sigmoid(gates[..., :D_MODEL])
        g_ssd = jax.nn.sigmoid(gates[..., D_MODEL:])
        merged = g_attn * (attn @ w_attn_out[l]) + g_ssd * (ssd @ w_ssd_out[l])
        x = x + gate1 * (merged @ w_o[l])

        h2 = rms_norm(x, norm2_w[l]) * (1.0 + scale2) + shift2
        ff = jnp.square(jax.nn.relu(h2 @ w_mlp1[l])) @ w_mlp2[l]
        x = x + gate2 * ff
    return x


DEPTH_2 = 2

N_A = max(1, DEPTH_2 // 2)
N_B = DEPTH_2 - N_A

D_RNN = 1280
RNN_BLOCKS = 10
RNN_BW = D_RNN // RNN_BLOCKS
CONV_WIDTH = 4
LRU_C = 8.0

N_HEADS = 8
QK_NOPE = 128
QK_ROPE = 64
V_DIM = 128
KV_RANK = 256
Q_RANK = 384
ATTN_SCALE = (QK_NOPE + QK_ROPE) ** -0.5


def rms_norm_2(x, g):
    xf = x.astype(jnp.float32)
    y = xf * lax.rsqrt(jnp.mean(xf * xf, axis=-1, keepdims=True) + EPS)
    return (y * g.astype(jnp.float32)).astype(x.dtype)

def rope_tables(seq_len):
    pos = jnp.arange(seq_len, dtype=jnp.float32)
    inv = ROPE_THETA ** (-jnp.arange(0, QK_ROPE, 2, dtype=jnp.float32) / QK_ROPE)
    ang = pos[:, None] * inv[None, :]
    return jnp.cos(ang), jnp.sin(ang)

def apply_rope(x, cos, sin):
    xf = x.astype(jnp.float32)
    x1, x2 = jnp.split(xf, 2, axis=-1)
    out = jnp.concatenate([x1 * cos - x2 * sin, x2 * cos + x1 * sin], axis=-1)
    return out.astype(x.dtype)

def causal_depthwise_conv(x, w, b):
    c = x.shape[-1]
    y = lax.conv_general_dilated(
        x, w[:, None, :].astype(x.dtype), window_strides=(1,),
        padding=[(CONV_WIDTH - 1, 0)], dimension_numbers=("NWC", "WIO", "NWC"),
        feature_group_count=c)
    return y + b

def _lin_combine(left, right):
    a1, b1 = left
    a2, b2 = right
    return a1 * a2, a2 * b1 + b2

def rglru_layer(x, norm_g, w_in, conv_w, conv_b, w_rg, b_rg, w_ig, b_ig, lam, w_out):
    bsz, seq, _ = x.shape
    h = rms_norm_2(x, norm_g)
    u = h @ w_in
    xb, gate = u[..., :D_RNN], u[..., D_RNN:]
    xb = causal_depthwise_conv(xb, conv_w, conv_b)
    xblk = xb.reshape(bsz, seq, RNN_BLOCKS, RNN_BW)
    r = jax.nn.sigmoid(jnp.einsum("bsnc,ncd->bsnd", xblk, w_rg).reshape(bsz, seq, D_RNN) + b_rg)
    i = jax.nn.sigmoid(jnp.einsum("bsnc,ncd->bsnd", xblk, w_ig).reshape(bsz, seq, D_RNN) + b_ig)
    log_a = -LRU_C * r.astype(jnp.float32) * jax.nn.softplus(-lam.astype(jnp.float32))
    a = jnp.exp(log_a)
    bterm = jnp.sqrt(-jnp.expm1(2.0 * log_a)) * (i * xb).astype(jnp.float32)
    _, hs = lax.associative_scan(_lin_combine, (a, bterm), axis=1)
    y = hs.astype(x.dtype) * jax.nn.silu(gate)
    return y @ w_out

def mla_shared_kv(x_stream, norm_kv, w_dkv, kv_norm, w_uk, w_uv, cos, sin):
    h = rms_norm_2(x_stream, norm_kv)
    ckr = h @ w_dkv
    c_kv = rms_norm_2(ckr[..., :KV_RANK], kv_norm)
    k_rope = apply_rope(ckr[..., KV_RANK:], cos[None], sin[None])
    k_nope = jnp.einsum("bsc,chd->bshd", c_kv, w_uk)
    v = jnp.einsum("bsc,chd->bshd", c_kv, w_uv)
    return k_nope, k_rope, v

def causal_block_attention(q_nope, q_rope, k_nope, k_rope, v):
    bsz, seq, nh, _ = q_nope.shape
    nb = seq // Q_BLOCK
    qn = q_nope.reshape(bsz, nb, Q_BLOCK, nh, QK_NOPE).transpose(1, 0, 2, 3, 4)
    qr = q_rope.reshape(bsz, nb, Q_BLOCK, nh, QK_ROPE).transpose(1, 0, 2, 3, 4)
    kpos = jnp.arange(seq)

    def one_block(args):
        qn_b, qr_b, bi = args
        s = jnp.einsum("bqhd,bkhd->bhqk", qn_b, k_nope, preferred_element_type=jnp.float32)
        s = s + jnp.einsum("bqhr,bkr->bhqk", qr_b, k_rope, preferred_element_type=jnp.float32)
        s = s * ATTN_SCALE
        qpos = bi * Q_BLOCK + jnp.arange(Q_BLOCK)
        mask = kpos[None, :] <= qpos[:, None]
        s = jnp.where(mask[None, None], s, -jnp.inf)
        p = jax.nn.softmax(s, axis=-1)
        return jnp.einsum("bhqk,bkhd->bqhd", p.astype(v.dtype), v)

    o = lax.map(one_block, (qn, qr, jnp.arange(nb)))
    return o.transpose(1, 0, 2, 3, 4).reshape(bsz, seq, nh, V_DIM)

def mla_layer(x, norm_g, w_in, q_norm, w_uq, w_out, k_nope, k_rope, v, cos, sin):
    bsz, seq, _ = x.shape
    h = rms_norm_2(x, norm_g)
    u = h @ w_in
    c_q = rms_norm_2(u[..., :Q_RANK], q_norm)
    gate = u[..., Q_RANK:]
    q = jnp.einsum("bsc,chd->bshd", c_q, w_uq)
    q_nope = q[..., :QK_NOPE]
    q_rope = apply_rope(q[..., QK_NOPE:], cos[None, :, None], sin[None, :, None])
    o = causal_block_attention(q_nope, q_rope, k_nope, k_rope, v)
    y = o.reshape(bsz, seq, N_HEADS * V_DIM) * jax.nn.silu(gate)
    return y @ w_out

def second_inputs(seed: int = 0) -> dict:
    key = jax.random.key(seed)
    ks = jax.random.split(key, 24)
    f32 = jnp.float32
    nrm = lambda k, shape, fan_in: jax.random.normal(k, shape, f32) * (fan_in ** -0.5)
    gain = lambda k, shape: 1.0 + 0.02 * jax.random.normal(k, shape, f32)
    small = lambda k, shape: 0.01 * jax.random.normal(k, shape, f32)

    u = jax.random.uniform(ks[8], (N_A, D_RNN), f32, 0.9, 0.999)
    a0 = u ** (1.0 / LRU_C)
    lam = jnp.log(a0) - jnp.log1p(-a0)

    return {
        "x": jax.random.normal(ks[0], (BATCH, SEQ, D_MODEL), f32),
        "norm_a": gain(ks[1], (N_A, D_MODEL)),
        "w_in_a": nrm(ks[2], (N_A, D_MODEL, 2 * D_RNN), D_MODEL),
        "conv_w": nrm(ks[3], (N_A, CONV_WIDTH, D_RNN), CONV_WIDTH),
        "conv_b": small(ks[4], (N_A, D_RNN)),
        "w_rg": nrm(ks[5], (N_A, RNN_BLOCKS, RNN_BW, RNN_BW), RNN_BW),
        "b_rg": small(ks[6], (N_A, D_RNN)),
        "w_ig": nrm(ks[7], (N_A, RNN_BLOCKS, RNN_BW, RNN_BW), RNN_BW),
        "b_ig": small(ks[9], (N_A, D_RNN)),
        "lru_lambda": lam,
        "w_out_a": nrm(ks[10], (N_A, D_RNN, D_MODEL), D_RNN),
        "norm_kv": gain(ks[11], (D_MODEL,)),
        "w_dkv": nrm(ks[12], (D_MODEL, KV_RANK + QK_ROPE), D_MODEL),
        "kv_norm": gain(ks[13], (KV_RANK,)),
        "w_uk": nrm(ks[14], (KV_RANK, N_HEADS, QK_NOPE), KV_RANK),
        "w_uv": nrm(ks[15], (KV_RANK, N_HEADS, V_DIM), KV_RANK),
        "norm_b": gain(ks[16], (N_B, D_MODEL)),
        "w_in_b": nrm(ks[17], (N_B, D_MODEL, Q_RANK + N_HEADS * V_DIM), D_MODEL),
        "q_norm": gain(ks[18], (N_B, Q_RANK)),
        "w_uq": nrm(ks[19], (N_B, Q_RANK, N_HEADS, QK_NOPE + QK_ROPE), Q_RANK),
        "w_out_b": nrm(ks[20], (N_B, N_HEADS * V_DIM, D_MODEL), N_HEADS * V_DIM),
        "final_norm": gain(ks[21], (D_MODEL,)),
    }

def second_block(x, norm_a, w_in_a, conv_w, conv_b, w_rg, b_rg, w_ig, b_ig, lru_lambda, w_out_a,
              norm_kv, w_dkv, kv_norm, w_uk, w_uv,
              norm_b, w_in_b, q_norm, w_uq, w_out_b, final_norm):
    seq = x.shape[1]
    cos, sin = rope_tables(seq)
    k_nope = k_rope = v = None
    for layer in range(DEPTH_2):
        if layer < N_A:
            x = x + rglru_layer(x, norm_a[layer], w_in_a[layer], conv_w[layer], conv_b[layer],
                                w_rg[layer], b_rg[layer], w_ig[layer], b_ig[layer],
                                lru_lambda[layer], w_out_a[layer])
        else:
            if layer == N_A:
                k_nope, k_rope, v = mla_shared_kv(x, norm_kv, w_dkv, kv_norm, w_uk, w_uv, cos, sin)
            j = layer - N_A
            x = x + mla_layer(x, norm_b[j], w_in_b[j], q_norm[j], w_uq[j], w_out_b[j],
                              k_nope, k_rope, v, cos, sin)
    return rms_norm_2(x, final_norm)


def setup_inputs(seed=0):
    out = dict(first_inputs(seed))
    for name, value in second_inputs(seed + 1).items():
        if name != "x":
            out[name + "_2"] = value
    return out


def reference(
    x, c, w_ada, b_ada, norm1_w, norm2_w, w_in, q_norm_w, k_norm_w, conv_w, conv_b, A_log,
    dt_bias, ssd_D, ssd_norm_w, w_attn_out, w_ssd_out, w_o, w_mlp1, w_mlp2, norm_a_2, w_in_a_2,
    conv_w_2, conv_b_2, w_rg_2, b_rg_2, w_ig_2, b_ig_2, lru_lambda_2, w_out_a_2, norm_kv_2,
    w_dkv_2, kv_norm_2, w_uk_2, w_uv_2, norm_b_2, w_in_b_2, q_norm_2, w_uq_2, w_out_b_2,
    final_norm_2,
):
    x = first_block(
        x, c, w_ada, b_ada, norm1_w, norm2_w, w_in, q_norm_w, k_norm_w, conv_w, conv_b, A_log,
        dt_bias, ssd_D, ssd_norm_w, w_attn_out, w_ssd_out, w_o, w_mlp1, w_mlp2,
    )
    return second_block(
        x, norm_a_2, w_in_a_2, conv_w_2, conv_b_2, w_rg_2, b_rg_2, w_ig_2, b_ig_2, lru_lambda_2,
        w_out_a_2, norm_kv_2, w_dkv_2, kv_norm_2, w_uk_2, w_uv_2, norm_b_2, w_in_b_2, q_norm_2,
        w_uq_2, w_out_b_2, final_norm_2,
    )


_drawn_inputs = setup_inputs


def setup_inputs(seed=0):
    import zlib

    import numpy as np

    out = dict(_drawn_inputs(seed))
    spreads = {}
    factors = {'norm1_w': 8.0,
     'norm2_w': 5.822,
     'q_norm_w': 8.0,
     'k_norm_w': 8.0,
     'conv_b': 8.0,
     'ssd_D': 8.0,
     'ssd_norm_w': 8.0,
     'norm_a_2': 4.027,
     'b_rg_2': 8.0,
     'b_ig_2': 8.0,
     'norm_kv_2': 8.0,
     'kv_norm_2': 8.0,
     'norm_b_2': 8.0,
     'q_norm_2': 8.0,
     'final_norm_2': 2.839}
    for name, (base, spread) in spreads.items():
        noise = np.random.default_rng([zlib.crc32(name.encode()), seed]).standard_normal(out[name].shape)
        drawn = base * np.exp(spread * noise) if base else spread * noise
        out[name] = __import__('jax').numpy.asarray(drawn.astype(out[name].dtype))
    for name, factor in factors.items():
        out[name] = (out[name] * factor).astype(out[name].dtype)
    return out
```

```python
from contextlib import ExitStack

import concourse.bass as bass
from concourse import mybir

F32 = mybir.dt.float32
F32R = mybir.dt.float32r
BF16 = mybir.dt.bfloat16
ALU = mybir.AluOpType
ACT = mybir.ActivationFunctionType
AX = mybir.AxisListType.X

P = 128
D_MODEL, SEQ = 1024, 512
N_Q, N_KV, HD = 16, 4, 64
D_INNER, N_GROUPS, D_STATE, N_SSD = 2048, 4, 128, 32
D_FF = 4096
D_RNN, RNN_BLOCKS = 1280, 10
N_HEADS, QK_NOPE, QK_ROPE, V_DIM, KV_RANK, Q_RANK = 8, 128, 64, 128, 256, 384
EPS = 1e-6
LRU_C = 8.0
LOG_TERMS = 8

KT = D_MODEL // P
NCH = SEQ // P
PAIRS = D_INNER // P
PPG = PAIRS // N_GROUPS
QT = N_Q * HD // P
KVT = N_KV * HD // P
FQ = D_FF // D_MODEL
RT = D_RNN // P
CKT, CQT = KV_RANK // P, Q_RANK // P
BPS = 8
SLAB = BPS * P
RING = 3
AHEAD = 2

_PRM = [("norm1", KT), ("norm2", KT), ("qn", 1), ("kn", 1), ("cw", 5 * 24), ("cb", 24), ("ssdD", PAIRS),
        ("ssdn", PAIRS), ("na", KT), ("cw2", 4 * RT), ("cb2", RT), ("brg", RT), ("big", RT), ("lam", RT),
        ("nkv", KT), ("kvn", CKT), ("nb", KT), ("qn2", CQT), ("fin", KT), ("bada", 6 * KT), ("c", KT)]
PCOL, _n = {}, 0
for _name, _w in _PRM:
    PCOL[_name] = (_n, _w)
    _n += _w
N_PRM = _n
CONV_TILES = 24


def plan():
    order, tiles, at = [], {}, 0

    def tile(name, blocks, advance=True):
        nonlocal at
        tiles[name] = (len(tiles), at, blocks)
        if advance:
            at += blocks
            order.append((name, blocks))

    tile(("dt",), KT // 2)
    order.append(("pad", BPS - KT // 2))
    at += BPS - KT // 2
    tile(("B", 0), KT)
    tile(("C", 0), KT)
    tile(("xs", 0), KT)
    tile(("z", 0), KT)
    for i in range(PAIRS):
        g = i // PPG
        if i + 1 < PAIRS:
            if (i + 1) % PPG == 0:
                tile(("B", g + 1), KT)
                tile(("C", g + 1), KT)
            tile(("xs", i + 1), KT)
            tile(("z", i + 1), KT)
        if i % PPG == 0 and i:
            for m in range(KT):
                tile(("so", g - 1, m), PPG)
    for m in range(KT):
        tile(("so", N_GROUPS - 1, m), PPG)
    for t in range(KVT):
        tile(("k", t), KT)
    for c in range(NCH):
        tile(("v", c), KT * KVT, advance=(c == NCH - 1))
    for t in range(QT):
        tile(("q", t), KT)
    for m in range(KT):
        for w in ("ga", "gs", "wa"):
            tile((w, m), KT)
    for m in range(KT):
        tile(("wo", m), KT)
    for f in range(FQ):
        for m in range(KT):
            tile(("m1", f, m), KT)
        for m in range(KT):
            tile(("m2", f, m), KT)
    for n in range(RT):
        tile(("xb", n), KT)
        if n:
            tile(("rg", n - 1), 1)
            tile(("ig", n - 1), 1)
    tile(("rg", RT - 1), 1)
    tile(("ig", RT - 1), 1)
    for n in range(RT):
        tile(("gt", n), KT)
    for m in range(KT):
        tile(("oa", m), RT)
    for t in range(CKT):
        tile(("ck", t), KT)
    tile(("kr",), KT)
    for t in range(CQT):
        tile(("cq", t), KT)
    for h in range(N_HEADS):
        tile(("qr", h), CQT)
        tile(("kn", h), CKT)
        tile(("qn", h), CQT)
        tile(("vh", h), CKT)
        tile(("gh", h), KT)
    for m in range(KT):
        tile(("ob", m), KT)
    if at % BPS:
        order.append(("pad", BPS - at % BPS))
        at += BPS - at % BPS
    return tiles, order, at // BPS


TILES, ORDER, N_SLABS = plan()
CONV = [n for n in TILES if n[0] in ("B", "C", "xs")]
CONV_AT = {n: q for q, n in enumerate(CONV)}
NORMS = ([("n1", KT), ("ssd", PAIRS)] + [(("k", t), 1) for t in range(KVT)] + [(("q", t), 1) for t in range(QT)]
         + [("n2", KT), ("na", KT), ("nkv", KT), ("ckv", CKT), ("cq", CQT), ("fin", KT)])
NORM_AT, STAT_AT, _n = {}, {}, 0
for _j, (_name, _w) in enumerate(NORMS):
    NORM_AT[_name], STAT_AT[_name] = _j, (_n, _w)
    _n += _w
ADA_W = 2 * D_MODEL
ADA_G = 3
SWAP = [i ^ 16 for i in range(32)]


def slab_of(name):
    return TILES[name][1] // BPS


LAST_TILE = {}
for _name in TILES:
    _, _at, _b = TILES[_name]
    for _s in range(_at // BPS, (_at + _b - 1) // BPS + 1):
        LAST_TILE[_s] = TILES[_name][0]


class Steps:

    def __init__(self, eng, sem):
        self.eng, self.sem, self.n = eng, sem, 0

    def __call__(self, ins):
        ins.then_inc(self.sem, 1)
        self.n += 1

    def settle(self):
        self.eng.wait_ge(self.sem, self.n)


def build(nc, d):
    with ExitStack() as ctx:
        stack = [ctx]

        def sb(name, shape, dt=F32):
            return stack[-1].enter_context(nc.sbuf_tensor(name, shape, dt))

        def sem(name):
            return ctx.enter_context(nc.semaphore(name))

        class Arena:

            def __enter__(self):
                stack.append(ExitStack())
                return self

            def __exit__(self, *e):
                stack.pop().close()

        raw = [sb(f"w_raw{b}", [P, SLAB]) for b in range(RING)]
        whi = [sb(f"w_hi{b}", [P, SLAB], F32R) for b in range(RING)]
        wlo = [sb(f"w_lo{b}", [P, SLAB], F32R) for b in range(RING)]
        xF = sb("x_stream", [P, KT, SEQ])
        aH, aL = sb("a_hi", [P, KT, SEQ], F32R), sb("a_lo", [P, KT, SEQ], F32R)
        bH, bL = sb("b_hi", [P, KT, SEQ], F32R), sb("b_lo", [P, KT, SEQ], F32R)
        prm = sb("params", [P, N_PRM])
        cst = sb("consts", [P, 5 * P])
        cstb = sb("consts_bf16", [P, 3 * P], BF16)
        tbc = sb("dt_bias_and_A_log", [P, 4 * N_SSD])
        small = sb("small", [P, 320])
        t = [sb(f"tmp{i}", [P, SEQ]) for i in range(6)]
        sq = [sb(f"sq{i}", [P, SEQ]) for i in range(2)]
        std, rstd, rs_ssd = sb("std", [P, SEQ]), sb("rstd", [P, SEQ]), sb("rstd_ssd", [P, SEQ])

        ident, trif, trib, ones, blk64 = (cst[:, i * P:(i + 1) * P] for i in range(5))
        identb, mask_kq, mask_qk = (cstb[:, i * P:(i + 1) * P] for i in range(3))

        def col(name, i=0, n=1):
            a = PCOL[name][0] + i
            return prm[:, a:a + n]

        modc, gain1, gain2 = small[:, 0:48], small[:, 48:56], small[:, 56:64]
        csl, cth, eps = small[:, 64:72], small[:, 72:80], small[:, 80:81]
        w05, cwh, hbr = small[:, 82:98], small[:, 98:242], small[:, 242:262]
        nsp, lt = small[:, 262:272], small[:, 272:312]
        mx = [small[:, 312:316], small[:, 316:320]]

        with Arena():
            piece = [sb(f"ada_piece{b}", [P, ADA_W]) for b in range(2)]
            acc = sb("ada_acc", [P, ADA_W])
        with Arena():
            csB = sb("cs_rows", [P, 4, SEQ])
            Ex = sb("C_decayed", [P, 4, SEQ])
            Dm = sb("M", [P, 4, SEQ])
            XS = [sb(n, [P, NCH, P]) for n in ("X_state_f", "X_state_b", "X_f", "X_b")]
            BF = [sb(f"B_feat{b}", [P, SEQ]) for b in range(2)]
            CF = [sb(f"C_feat{b}", [P, SEQ]) for b in range(2)]
            BT = sb("B_tok", [P, NCH, P])
            CB = [sb(n, [P, SEQ]) for n in ("CB_f", "CB_b")]
            prev = sb("states", [P, 2, 3, P])
            xsF = [sb(f"x_feat{b}", [P, SEQ]) for b in range(2)]
            R2 = 2 * N_SSD
            dtT, csT, aT, wS, decB, dtw = (sb(n, [P, NCH, R2]) for n in ("dt", "cs", "a", "dt_decay", "chunk_decay",
                                                                          "dt_work"))
            dtx = sb("dt_work2", [P, NCH, R2])
            csF = sb("cs_feat", [R2, SEQ])
        with Arena():
            rope1 = sb("rope1_table", [P, 2, SEQ])
            kH = [sb(f"k_hi{g}", [HD + 1, SEQ], F32R) for g in range(N_KV)]
            kL = [sb(f"k_lo{g}", [HD + 1, SEQ], F32R) for g in range(N_KV)]
            qH = [sb(f"q_hi{b}", [HD + 1, SEQ], F32R) for b in range(4)]
            qL = [sb(f"q_lo{b}", [HD + 1, SEQ], F32R) for b in range(4)]
            vv = sb("v_and_ones", [P, NCH, N_KV, P])
            PT = sb("probs", [P, NCH, SEQ])
        with Arena():
            cH, cL = sb("c_hi", [P, KT, SEQ], F32R), sb("c_lo", [P, KT, SEQ], F32R)
            piece2 = [sb(f"ada2_piece{b}", [P, ADA_W]) for b in range(2)]
            acc2 = sb("ada2_acc", [P, ADA_W])
        with Arena():
            xacc = [sb(f"xb_conv{b}", [P, SEQ]) for b in range(2)]
            xH = [sb(f"xb_hi{b}", [P, SEQ], F32R) for b in range(2)]
            xL = [sb(f"xb_lo{b}", [P, SEQ], F32R) for b in range(2)]
            t2 = sb("tanh_half_log_a", [P, RT, SEQ])
            xbi = sb("gated_x", [P, RT, SEQ])
            yH, yL = sb("y_hi", [P, RT - KT, SEQ], F32R), sb("y_lo", [P, RT - KT, SEQ], F32R)
        with Arena():
            rope2 = sb("rope2_table", [P, SEQ])
            ckH, ckL = sb("ckv_hi", [P, CKT, SEQ], F32R), sb("ckv_lo", [P, CKT, SEQ], F32R)
            cqH, cqL = sb("cq_hi", [P, CQT, SEQ], F32R), sb("cq_lo", [P, CQT, SEQ], F32R)
            krH, krL = sb("krope_hi", [QK_ROPE + 1, SEQ], F32R), sb("krope_lo", [QK_ROPE + 1, SEQ], F32R)
            qrH = [sb(f"qrope_hi{b}", [QK_ROPE + 1, SEQ], F32R) for b in range(2)]
            qrL = [sb(f"qrope_lo{b}", [QK_ROPE + 1, SEQ], F32R) for b in range(2)]
            knH, knL, qnH, qnL = ([sb(f"{n}{b}", [P, SEQ], F32R) for b in range(2)]
                                  for n in ("knope_hi", "knope_lo", "qnope_hi", "qnope_lo"))
            vm = [sb(f"v_tok{b}", [P, NCH, V_DIM]) for b in range(2)]
            PT2 = sb("probs2", [P, NCH, SEQ])
            ckf = PT2[:, 0:CQT, :]

        bank = [ctx.enter_context(nc.psum_tensor(f"bank{i}", [P, SEQ], F32)) for i in range(8)]
        G, PST = bank[0:2], bank[2]
        XT, STF, STB, YP, PM = bank[3:8]
        M, S, OP, DEN = bank[3:5], bank[5:7], bank[7], bank[2]
        ADA = bank[7]
        zth = [t[4][:, :], t[5][:, :]]
        t_yz = [xsF[0][:, :], xsF[1][:, :]]

        s_in, s_x, s_rope, s_x2, s_out = sem("inputs_in"), sem("x_in"), sem("rope_in"), sem("x_again"), sem("out_done")
        w_in = [sem(f"slab_in{b}") for b in range(RING)]
        hi_done, lo_done = sem("slab_hi"), sem("slab_lo")
        gemm_done = sem("tile_done")
        evac = [sem(f"tile_evacuated{b}") for b in range(2)]
        v_step, a_step = sem("vector_step"), sem("scalar_step")
        vec_prep = sem("vector_prep")
        ada_in = [sem(f"ada_in{b}") for b in range(2)]
        ada_acc, ada_red, mod_ready = sem("ada_added"), sem("ada_reduced"), sem("mod_ready")
        c_th = sem("silu_c")
        sq_ready, stat_mm, std_ready, rstd_ready = sem("square"), sem("square_summed"), sem("std"), sem("rstd")
        nfull = sem("normed")
        hiA, hiB, hiC, hiY, hiK, hiX = (sem(f"hi_{n}") for n in "ABCYKX")
        rdyA, rdyB, rdyC, rdyY, rdyK, rdyX = (sem(f"ready_{n}") for n in "ABCYKX")
        sp_x, sp_e = sem("softplus_arg"), sem("softplus_exp")
        a_ready, cs_done, cs_ev, tot_e, cs_sb, cs_dram = (sem(n) for n in ("dt_a", "cs_psum", "cs_tok", "decay_arg",
                                                                           "cs_rows_sb", "cs_rows_dram"))
        wdec, decb = sem("decay_state"), sem("decay_chunk")
        csb_in, e_ready, d_ready, ed_ready = sem("cs_in"), sem("C_decay"), sem("M_arg"), sem("M_exp")
        conv0, conv_th, conv_done, z_th = sem("conv_first"), sem("conv_tanh"), sem("conv_done"), sem("z_tanh")
        xt_done, xs_sc, bt_done, bt_ev, cb_done, cb_ev = (sem(n) for n in ("x_turned", "x_scaled", "B_turned", "B_tok",
                                                                           "CB_psum", "CB_masked"))
        m_ready, ce_ready, st_done, rec_done = sem("M_ready"), sem("CE_ready"), sem("states_psum"), sem("states_run")
        y_done, y_ev, yz_ready = sem("y_psum"), sem("y_out"), sem("y_gated")
        k_ready, q_ready, fills = sem("k_ready"), sem("q_ready"), sem("fills")
        rope_done = sem("roped")
        qk_done, exp_done, pv_done, o_ev = sem("scores"), sem("probs"), sem("pv"), sem("attn_out")
        mx_done, mx_red, rows_done, row_ready = sem("max_scores"), sem("max_taken"), sem("max_row"), sem("max_row_in_q")
        mrg = sem("merged")
        lam_e, lam_l = sem("lam_exp"), sem("lam_ln")
        c20, rg_th, ig_th, t2_done, xbi_done, s_done, xbs_done = (sem(n) for n in (
            "conv2_first", "rg_tanh", "ig_tanh", "tanh_half", "gated_x", "sqrt_done", "gated_x_scaled"))
        g_th, y2_ready = sem("gate_tanh"), sem("y2_ready")
        ck_x = sem("c_normed")
        kr_ready, kn_hi, qr_ready, qn_hi, gh_th = (sem(n) for n in (
            "krope", "kn_hi", "qrope", "qn_hi", "gate2_tanh"))
        qk2, exp2, pv2, o2, mxd2, mxr2, rows2, row2, yb = (sem(n) for n in (
            "scores2", "probs2", "pv2", "attn2_out", "max2_scores", "max2_taken", "max2_row", "max2_row_in_q", "attn2_gated"))
        fin_ready = sem("final_ready")
        rope2_in = sem("rope2_in")

        def wait_tile(eng, name):
            eng.wait_ge(gemm_done, TILES[name][0] + 1)

        def wait_evac(eng, name):
            n = TILES[name][0]
            eng.wait_ge(evac[n % 2], n // 2 + 1)

        def gb(name):
            return G[TILES[name][0] % 2]

        def inc_evac(ins, name):
            ins.then_inc(evac[TILES[name][0] % 2], 1)

        def r32(ap):
            return ap.bitcast(F32)

        block = ctx.enter_context(nc.Block())

        @block.sync
        def _(sp):
            for n, dst in (("prm", prm), ("cst", cst), ("cstb", cstb), ("tb", tbc)):
                src = d[n].partition_broadcast(P) if n == "tb" else d[n]
                sp.dma_start(dst[:, :], src).then_inc(s_in, 16)
            for p in range(KT):
                if p >= 2:
                    sp.wait_ge(ada_acc, p - 1)
                sp.dma_start(piece[p % 2][:, :], d["ada"][p]).then_inc(ada_in[p % 2], 16)
                if p == 1:
                    sp.dma_start(xF[:, :, :], d["x"]).then_inc(s_x, 16)
            for s in range(N_SLABS):
                if s >= RING:
                    sp.wait_ge(lo_done, s - RING + 1)
                sp.dma_start(raw[s % RING][:, :], d["ws"][s]).then_inc(w_in[s % RING], 16)
            for m in range(KT):
                sp.wait_ge(fin_ready, m + 1)
                sp.dma_start(d["out"][m], xF[:, m, :]).then_inc(s_out, 16)
            sp.wait_ge(s_out, 16 * KT)

        @block.gpsimd
        def _(pool):
            for s in range(N_SLABS):
                pool.wait_ge(hi_done, s + 1)
                nc.gpsimd.tensor_tensor(wlo[s % RING][:, :], raw[s % RING][:, :], r32(whi[s % RING][:, :]),
                                        ALU.subtract).then_inc(lo_done, 1)

        @block.scalar
        def _(act):
            a = Steps(act, a_step)
            A = nc.scalar.activation
            state = {"hi": 0}

            def hi_upto(s):
                while state["hi"] <= min(s, N_SLABS - 1):
                    n = state["hi"]
                    act.wait_ge(w_in[n % RING], 16 * (n // RING + 1))
                    if n >= RING:
                        act.wait_ge(gemm_done, LAST_TILE.get(n - RING, 0) + 1)
                    A(whi[n % RING][:, :], raw[n % RING][:, :], ACT.Copy).then_inc(hi_done, 1)
                    state["hi"] += 1

            def tile_in(name):
                hi_upto(slab_of(name) + AHEAD)
                wait_tile(act, name)

            def square(norm, k, src, scale=1.0):
                n = STAT_AT[norm][0] + k
                if n >= 2:
                    act.wait_ge(stat_mm, n - 1)
                A(sq[n % 2][:, :], src, ACT.Square, scale=scale).then_inc(sq_ready, 1)

            def root(norm, scale):
                j, (n, w) = NORM_AT[norm], STAT_AT[norm]
                act.wait_ge(stat_mm, n + w)
                if j:
                    act.wait_ge(rstd_ready, j)
                A(std[:, :], PST[:, :], ACT.Sqrt, bias=eps, scale=scale).then_inc(std_ready, 1)

            act.wait_ge(s_in, 64)
            act.wait_ge(vec_prep, 1)
            A(cth, col("c", 0, KT), ACT.Tanh, scale=0.5).then_inc(c_th, 1)
            act.wait_ge(s_x, 16)
            for k in range(KT):
                square("n1", k, xF[:, k, :])
            root("n1", 1.0 / D_MODEL)
            hi_upto(AHEAD)
            for k in range(KT):
                act.wait_ge(nfull, k + 1)
                A(aH[:, k, :], t[k % 2][:, :], ACT.Identity, bias=modc[:, k:k + 1]).then_inc(hiA, 1)

            def conv_act(name):
                q = CONV_AT[name]
                i = {"xs": name[1], "B": 16 + name[1], "C": 20 + name[1]}[name[0]]
                tile_in(name)
                if q >= 2:
                    act.wait_ge(conv_done, q - 1)
                A(t[q % 2][:, :], gb(name)[:, :], ACT.Identity, scale=cwh[:, 2 * 24 + i:2 * 24 + i + 1],
                  bias=cwh[:, 5 * 24 + i:5 * 24 + i + 1]).then_inc(conv0, 1)
                wait_evac(act, name)
                A(t[2 + q % 2][:, :], t[q % 2][:, :], ACT.Tanh).then_inc(conv_th, 1)

            def z_act(i):
                tile_in(("z", i))
                if i >= 2:
                    act.wait_ge(yz_ready, i - 1)
                A(zth[i % 2], gb(("z", i))[:, :], ACT.Tanh, scale=0.5).then_inc(z_th, 1)

            tile_in(("dt",))
            act.wait_ge(sp_x, 1)
            A(dtw[:, :, :], dtw[:, :, :], ACT.Exp).then_inc(sp_e, 1)
            A(tbc[:, R2:2 * R2], tbc[:, R2:2 * R2], ACT.Exp).then_inc(sp_e, 1)
            act.wait_ge(lam_e, 1)
            A(lt[:, RT:2 * RT], lt[:, 0:RT], ACT.Exp).then_inc(lam_l, 1)
            conv_act(("B", 0))
            conv_act(("C", 0))
            act.wait_ge(cs_done, 1)
            A(csF[:, :], YP[0:R2, :], ACT.Copy).then_inc(cs_sb, 1)
            A(decB[:, :, :], STF[:, 0:NCH * R2], ACT.Exp).then_inc(decb, 1)
            act.wait_ge(cs_sb, 1)
            act.dma_start(d["cs"], csF[:, :]).then_inc(cs_dram, 16)
            act.wait_ge(tot_e, 1)
            A(wS[:, :, :], dtw[:, :, :], ACT.Exp).then_inc(wdec, 1)

            def load_cs(i):
                src = d["cs"].rearrange("(d h) n -> d h n", d=2)[:, 2 * i:2 * i + 2, :]
                act.dma_start(csB[:, :, :].rearrange("p (d h) n -> p d h n", d=2),
                              src.partition_broadcast(P)).then_inc(csb_in, 16)

            act.wait_ge(cs_dram, 16)
            load_cs(0)

            conv_act(("xs", 0))
            z_act(0)
            for i in range(PAIRS):
                g = i // PPG
                if i % PPG == 0:
                    act.wait_ge(bt_done, g + 1)
                    A(BT[:, :, :], PM[:, :], ACT.Copy).then_inc(bt_ev, 1)
                act.wait_ge(csb_in, 16 * (i + 1))
                if i:
                    act.wait_ge(y_done, i)
                A(Ex[:, :, :], csB[:, :, :], ACT.Exp).then_inc(e_ready, 1)
                act.wait_ge(d_ready, i + 1)
                A(Dm[:, :, :], Dm[:, :, :], ACT.Exp).then_inc(ed_ready, 1)
                if i + 1 < PAIRS:
                    act.wait_ge(e_ready, i + 1)
                    load_cs(i + 1)
                    if (i + 1) % PPG == 0:
                        conv_act(("B", g + 1))
                        conv_act(("C", g + 1))
                    conv_act(("xs", i + 1))
                    z_act(i + 1)
                act.wait_ge(yz_ready, i + 1)
                square("ssd", i, t_yz[i % 2], 0.5)
                A(bH[:, i % KT, :], t_yz[i % 2], ACT.Copy, scale=w05[:, i:i + 1]).then_inc(hiB, 1)
                if i % PPG == 0 and i:
                    hi_upto(slab_of(("so", g - 1, KT - 1)))
            hi_upto(slab_of(("so", N_GROUPS - 1, KT - 1)) + AHEAD)
            root("ssd", 1.0 / D_INNER)

            act.wait_ge(y_done, PAIRS)
            act.wait_ge(ce_ready, PAIRS)
            act.dma_start(rope1[:, :, :], d["rope1"]).then_inc(s_rope, 16)

            def qk_copy(name, w, j):
                tile_in(name)
                square(name, 0, gb(name)[:, :])
                if j >= 2:
                    act.wait_ge(rope_done, j - 1)
                inc_evac(A(t[j % 2][:, :], gb(name)[:, :], ACT.Copy, scale=w), name)

            for j in range(KVT):
                qk_copy(("k", j), col("kn"), j)
                root(("k", j), 1.0)
            for c in range(NCH):
                tile_in(("v", c))
                if c == 0:
                    act.wait_ge(y_done, PAIRS)
                inc_evac(A(vv[:, c, :, 0:HD], gb(("v", c))[:, 0:N_KV * HD].rearrange("p (g d) -> p g d", g=N_KV),
                           ACT.Copy), ("v", c))
            qk_copy(("q", 0), col("qn"), KVT)
            root(("q", 0), 1.0)

            def max_row(h):
                act.wait_ge(rows_done, h + 1)
                A(qH[h % 4][HD:HD + 1, :], M[0][0:1, :], ACT.Copy, scale=-1.0).then_inc(row_ready, 1)

            max_row(0)
            for h in range(N_Q):
                u = h // 2
                for c in range(NCH):
                    n = NCH * h + c
                    act.wait_ge(qk_done, n + 1)
                    if h:
                        act.wait_ge(pv_done, n - NCH + 1)
                    A(PT[:, c, :], S[n % 2][:, :], ACT.Exp, scale=HD ** -0.5).then_inc(exp_done, 1)
                if h % 2 == 0 and u + 1 < QT:
                    qk_copy(("q", u + 1), col("qn"), KVT + u + 1)
                if h + 1 < N_Q:
                    max_row(h + 1)
                if h % 2 == 0 and u + 1 < QT:
                    root(("q", u + 1), 1.0)
                if h % 2:
                    act.wait_ge(o_ev, h + 1)
                    if u == 0:
                        wait_tile(act, ("so", N_GROUPS - 1, KT - 1))
                    A(bH[:, u, :], t[4 + u % 2][:, :], ACT.Copy).then_inc(hiB, 1)

            def ada2_load(p):
                if p >= KT + 2:
                    act.wait_ge(ada_acc, p - 1)
                act.dma_start(piece2[p % 2][:, :], d["ada"][p]).then_inc(ada_in[p % 2], 16)

            act.wait_ge(pv_done, NCH * N_Q)
            act.wait_ge(rope_done, KVT + QT)
            ada2_load(KT)
            ada2_load(KT + 1)
            for m in range(KT):
                tile_in(("ga", m))
                if m >= 2:
                    act.wait_ge(mrg, m - 1)
                inc_evac(A(t[m % 2][:, :], gb(("ga", m))[:, :], ACT.Tanh, scale=0.5), ("ga", m))
                tile_in(("gs", m))
                inc_evac(A(t[2 + m % 2][:, :], gb(("gs", m))[:, :], ACT.Tanh, scale=0.5), ("gs", m))
                hi_upto(slab_of(("wa", m)) + AHEAD)
                act.wait_ge(mrg, m + 1)
                A(cH[:, m, :], t[4 + m % 2][:, :], ACT.Copy, scale=0.5).then_inc(hiC, 1)
                for p in (KT + 2 * m + 2, KT + 2 * m + 3):
                    if p < ADA_G * KT:
                        ada2_load(p)
            act.dma_start(xF[:, :, :], d["x"]).then_inc(s_x2, 16)
            for m in range(KT):
                hi_upto(slab_of(("wo", m)) + AHEAD)
                wait_evac(act, ("wo", m))
                square("n2", m, xF[:, m, :])
            root("n2", 1.0 / D_MODEL)
            for k in range(KT):
                act.wait_ge(nfull, KT + k + 1)
                A(aH[:, k, :], t[k % 2][:, :], ACT.Identity, bias=modc[:, 3 * KT + k:3 * KT + k + 1]).then_inc(hiA, 1)

            for f in range(FQ):
                for m in range(KT):
                    n = KT * f + m
                    tile_in(("m1", f, m))
                    if n >= 2:
                        act.wait_ge(rdyB, 24 + n - 1)
                    inc_evac(A(t[2 + n % 2][:, :], gb(("m1", f, m))[:, :], ACT.Relu), ("m1", f, m))
                    wait_evac(act, ("m1", f, m))
                    A(bH[:, m, :], t[2 + n % 2][:, :], ACT.Square).then_inc(hiB, 1)
                for m in range(KT):
                    hi_upto(slab_of(("m2", f, m)) + AHEAD)
                    if f == FQ - 1:
                        wait_evac(act, ("m2", f, m))
                        square("na", m, xF[:, m, :])

            root("na", 1.0 / D_MODEL)
            for k in range(KT):
                act.wait_ge(nfull, 2 * KT + k + 1)
                A(aH[:, k, :], t[k % 2][:, :], ACT.Copy).then_inc(hiA, 1)

            def gates(n):
                tile_in(("rg", n))
                if n >= 1:
                    act.wait_ge(t2_done, n)
                else:
                    act.wait_ge(hiB, 24 + KT * FQ)
                inc_evac(A(t[2][:, :], gb(("rg", n))[:, :], ACT.Tanh, scale=0.5, bias=hbr[:, n:n + 1]), ("rg", n))
                tile_in(("ig", n))
                if n >= 2:
                    act.wait_ge(xbi_done, n - 1)
                inc_evac(A(t[4 + n % 2][:, :], gb(("ig", n))[:, :], ACT.Tanh, scale=0.5,
                           bias=hbr[:, RT + n:RT + n + 1]), ("ig", n))
                wait_evac(act, ("rg", n))
                A(t2[:, n, :], t[2][:, :], ACT.Tanh, scale=nsp[:, n:n + 1], bias=nsp[:, n:n + 1]).then_inc(t2_done, 1)

            act.wait_ge(lam_e, 2)
            for n in range(RT):
                tile_in(("xb", n))
                if n >= 2:
                    act.wait_ge(xbi_done, n - 1)
                A(xacc[n % 2][:, :], gb(("xb", n))[:, :], ACT.Identity, scale=col("cw2", 3 * RT + n),
                  bias=col("cb2", n)).then_inc(c20, 1)
                wait_evac(act, ("xb", n))
                if n >= 2:
                    wait_tile(act, ("ig", n - 2))
                A(xH[n % 2][:, :], xacc[n % 2][:, :], ACT.Copy).then_inc(hiX, 1)
                if n:
                    gates(n - 1)
            gates(RT - 1)
            hi_upto(slab_of(("gt", 0)) + 1)
            act.wait_ge(t2_done, RT)
            for n in range(RT):
                if n >= 2:
                    act.wait_ge(xbs_done, n - 1)
                A(t[2 + n % 2][:, :], t2[:, n, :], ACT.Sqrt, scale=-1.0).then_inc(s_done, 1)
            for n in range(RT):
                tile_in(("gt", n))
                A(t[4 + n % 2][:, :], gb(("gt", n))[:, :], ACT.Tanh, scale=0.5).then_inc(g_th, 1)
                act.wait_ge(y2_ready, n + 1)
                dst, ev = (bH[:, n, :], hiB) if n < KT else (yH[:, n - KT, :], hiY)
                A(dst, t[n % 2][:, :], ACT.Copy, scale=0.5).then_inc(ev, 1)
            for m in range(KT):
                hi_upto(slab_of(("oa", m)) + AHEAD)
                wait_evac(act, ("oa", m))
                square("nkv", m, xF[:, m, :])

            act.wait_ge(xbs_done, RT)
            act.wait_ge(rdyY, RT - KT)
            act.dma_start(rope2[:, :], d["rope2"]).then_inc(rope2_in, 16)
            root("nkv", 1.0 / D_MODEL)
            for k in range(KT):
                act.wait_ge(nfull, 3 * KT + k + 1)
                A(aH[:, k, :], t[k % 2][:, :], ACT.Copy).then_inc(hiA, 1)
            for k in range(KT):
                act.wait_ge(nfull, 4 * KT + k + 1)
                A(bH[:, k, :], t[k % 2][:, :], ACT.Copy).then_inc(hiB, 1)
            for i in range(CKT):
                tile_in(("ck", i))
                square("ckv", i, gb(("ck", i))[:, :])
                inc_evac(A(ckf[:, i, :], gb(("ck", i))[:, :], ACT.Copy), ("ck", i))
            root("ckv", 1.0 / KV_RANK)
            for i in range(CKT):
                act.wait_ge(ck_x, i + 1)
                A(ckH[:, i, :], t[i % 2][:, :], ACT.Copy).then_inc(hiK, 1)
            hi_upto(slab_of(("kr",)) + AHEAD)
            for i in range(CQT):
                tile_in(("cq", i))
                square("cq", i, gb(("cq", i))[:, :])
                if i < CKT:
                    act.wait_ge(ck_x, i + 1)
                inc_evac(A(ckf[:, i, :], gb(("cq", i))[:, :], ACT.Copy), ("cq", i))
            root("cq", 1.0 / Q_RANK)
            for i in range(CQT):
                act.wait_ge(ck_x, CKT + i + 1)
                A(cqH[:, i, :], t[i % 2][:, :], ACT.Copy).then_inc(hiK, 1)

            def head_gemms1(h):
                hi_upto(slab_of(("qn", h)) + AHEAD)
                tile_in(("kn", h))
                A(knH[h % 2][:, :], gb(("kn", h))[:, :], ACT.Copy).then_inc(kn_hi, 1)
                tile_in(("qn", h))
                A(qnH[h % 2][:, :], gb(("qn", h))[:, :], ACT.Copy).then_inc(qn_hi, 1)

            def head_gemms2(h):
                tile_in(("vh", h))
                inc_evac(A(vm[h % 2][:, :, :], gb(("vh", h))[:, :], ACT.Copy), ("vh", h))
                tile_in(("gh", h))
                A(t[4 + h % 2][:, :], gb(("gh", h))[:, :], ACT.Tanh, scale=0.5).then_inc(gh_th, 1)

            def max_row2(h):
                act.wait_ge(rows2, h + 1)
                A(qrH[h % 2][QK_ROPE:QK_ROPE + 1, :], M[0][0:1, :], ACT.Copy, scale=-1.0).then_inc(row2, 1)

            head_gemms1(0)
            head_gemms2(0)
            max_row2(0)
            for h in range(N_HEADS):
                for c in range(NCH):
                    n = NCH * h + c
                    act.wait_ge(qk2, n + 1)
                    if h:
                        act.wait_ge(pv2, n - NCH + 1)
                    A(PT2[:, c, c * P:SEQ], S[n % 2][:, c * P:SEQ], ACT.Exp,
                      scale=(QK_NOPE + QK_ROPE) ** -0.5).then_inc(exp2, 1)
                if h + 1 < N_HEADS:
                    head_gemms1(h + 1)
                    head_gemms2(h + 1)
                    max_row2(h + 1)
                act.wait_ge(yb, h + 1)
                A(aH[:, h, :], t[2][:, :], ACT.Copy, scale=0.5).then_inc(hiA, 1)
            for m in range(KT):
                hi_upto(slab_of(("ob", m)) + AHEAD)
                wait_evac(act, ("ob", m))
                square("fin", m, xF[:, m, :])
            root("fin", 1.0 / D_MODEL)

        @block.tensor
        def _(pe):
            mm = nc.tensor.matmul

            def start(name):
                n = TILES[name][0]
                if n >= 2:
                    pe.wait_ge(evac[n % 2], n // 2)

            def weights(name):
                _, at, blocks = TILES[name]
                for n in range(at, at + blocks):
                    if n == at or n % BPS == 0:
                        pe.wait_ge(lo_done, n // BPS + 1)
                    yield n // BPS % RING, (n % BPS) * P

            def split_mm(out, lh, ll, rh, rl, first, last):
                mm(out, lh, rh, start=first, stop=False)
                mm(out, lh, rl, start=False, stop=False)
                return mm(out, ll, rh, start=False, stop=last)

            def feature_tile(name, hi, lo, ready=None):
                start(name)
                blocks = TILES[name][2]
                for k, (b, o) in enumerate(weights(name)):
                    if ready:
                        pe.wait_ge(ready[0], ready[1] + k + 1)
                    ins = split_mm(gb(name)[:, :], whi[b][:, o:o + P], wlo[b][:, o:o + P], hi(k), lo(k), k == 0,
                                   k == blocks - 1)
                ins.then_inc(gemm_done, 1)

            def in_a(k):
                return aH[:, k, :]

            def in_a_lo(k):
                return aL[:, k, :]

            def in_b(k):
                return bH[:, k, :]

            def in_b_lo(k):
                return bL[:, k, :]

            def stat(norm, k, ones_=None):
                j, (n0, w) = NORM_AT[norm], STAT_AT[norm]
                n = n0 + k
                pe.wait_ge(sq_ready, n + 1)
                if k == 0 and j:
                    pe.wait_ge(std_ready, j)
                mm(PST[:, :], ones if ones_ is None else ones_, sq[n % 2][:, :], start=(k == 0),
                   stop=(k == w - 1)).then_inc(stat_mm, 1)

            def ada_reduce(src, j):
                pe.wait_ge(ada_acc, KT * (j + 1))
                if j:
                    pe.wait_ge(mod_ready, j)
                for b in range(ADA_W // P):
                    ins = mm(ADA[:, b:b + 1], src[:, b * P:(b + 1) * P], ones[:, 0:1], start=True, stop=True)
                ins.then_inc(ada_red, 1)

            pe.wait_ge(s_in, 64)
            for k in range(KT):
                stat("n1", k)
            ada_reduce(acc, 0)

            name = ("dt",)
            for k in range(KT):
                pe.wait_ge(rdyA, k + 1)
            blk = list(weights(name))
            for c in range(NCH):
                for k in range(KT):
                    b, o = blk[k // 2]
                    o += k % 2 * R2
                    ins = split_mm(gb(name)[:, c * R2:(c + 1) * R2], aH[:, k, c * P:(c + 1) * P],
                                   aL[:, k, c * P:(c + 1) * P], whi[b][:, o:o + R2], wlo[b][:, o:o + R2], k == 0,
                                   k == KT - 1)
            ins.then_inc(gemm_done, 1)
            for n in (("B", 0), ("C", 0)):
                feature_tile(n, in_a, in_a_lo)
            pe.wait_ge(a_ready, 1)
            for c in range(NCH):
                for dd, tri in ((0, trif), (1, trib)):
                    r = slice(dd * N_SSD, (dd + 1) * N_SSD)
                    mm(STB[:, c * R2 + dd * N_SSD:c * R2 + (dd + 1) * N_SSD], tri, aT[:, c, r], start=True, stop=True)
                    mm(YP[r, c * P:(c + 1) * P], aT[:, c, r], tri, start=True, stop=True)
                ins = mm(STF[:, c * R2:(c + 1) * R2], ones, aT[:, c, :], start=True, stop=True)
            ins.then_inc(cs_done, 1)
            feature_tile(("xs", 0), in_a, in_a_lo)
            feature_tile(("z", 0), in_a, in_a_lo)
            pe.wait_ge(decb, 1)
            pe.wait_ge(tot_e, 1)

            for i in range(PAIRS):
                g, pg = i // PPG, i % PPG
                pe.wait_ge(conv_done, CONV_AT[("xs", i)] + 1)
                if i:
                    pe.wait_ge(xs_sc, i)
                for c in range(NCH):
                    ins = nc.tensor.transpose(XT[:, c * P:(c + 1) * P], xsF[i % 2][:, c * P:(c + 1) * P], ident)
                ins.then_inc(xt_done, 1)
                if pg == 0:
                    pe.wait_ge(conv_done, CONV_AT[("C", g)] + 1)
                    if g:
                        pe.wait_ge(bt_ev, g)
                        pe.wait_ge(rec_done, i)
                    for c in range(NCH):
                        ins = nc.tensor.transpose(PM[:, c * P:(c + 1) * P], BF[g % 2][:, c * P:(c + 1) * P], ident)
                    ins.then_inc(bt_done, 1)
                    for c in range(NCH):
                        w = slice(c * P, (c + 1) * P)
                        ins = mm(STF[:, w], BF[g % 2][:, w], CF[g % 2][:, w], start=True, stop=True)
                    ins.then_inc(cb_done, 1)
                if i:
                    stat("ssd", i - 1)
                if i + 1 < PAIRS:
                    if (i + 1) % PPG == 0:
                        feature_tile(("B", g + 1), in_a, in_a_lo)
                        feature_tile(("C", g + 1), in_a, in_a_lo)
                    feature_tile(("xs", i + 1), in_a, in_a_lo)
                pe.wait_ge(xs_sc, i + 1)
                pe.wait_ge(bt_ev, g + 1)
                pe.wait_ge(cb_ev, 2 * (g + 1))
                if i:
                    pe.wait_ge(rec_done, i)
                for c in range(NCH - 1):
                    mm(STF[:, c * P:(c + 1) * P], BT[:, c, :], XS[0][:, c, :], start=True, stop=True)
                    ins = mm(STB[:, c * P:(c + 1) * P], BT[:, c + 1, :], XS[1][:, c + 1, :], start=True, stop=True)
                ins.then_inc(st_done, 1)
                if i + 1 < PAIRS:
                    feature_tile(("z", i + 1), in_a, in_a_lo)
                pe.wait_ge(m_ready, 2 * (i + 1))
                pe.wait_ge(ce_ready, i + 1)
                pe.wait_ge(rec_done, i + 1)
                if i:
                    pe.wait_ge(y_ev, i)
                for hh in range(2):
                    hp = slice(hh * HD, (hh + 1) * HD)
                    for c in range(NCH):
                        w = slice(c * P, (c + 1) * P)
                        out = YP[hp, w]
                        mm(out, XS[2][:, c, hp], Dm[:, hh, w], start=True, stop=False)
                        if c:
                            mm(out, prev[:, 0, c - 1, hp], Ex[:, hh, w], start=False, stop=False)
                        if c < NCH - 1:
                            mm(out, prev[:, 1, c, hp], Ex[:, 2 + hh, w], start=False, stop=False)
                        ins = mm(out, XS[3][:, c, hp], Dm[:, 2 + hh, w], start=False, stop=True)
                ins.then_inc(y_done, 1)
                if pg == 0 and i:
                    for m in range(KT):
                        feature_tile(("so", g - 1, m), lambda k: bH[:, (g - 1) % 2 * PPG + k, :],
                                     lambda k: bL[:, (g - 1) % 2 * PPG + k, :], (rdyB, PPG * (g - 1)))
            stat("ssd", PAIRS - 1)
            g = N_GROUPS
            for m in range(KT):
                feature_tile(("so", g - 1, m), lambda k: bH[:, (g - 1) % 2 * PPG + k, :],
                             lambda k: bL[:, (g - 1) % 2 * PPG + k, :], (rdyB, PPG * (g - 1)))

            for j in range(KVT):
                feature_tile(("k", j), in_a, in_a_lo)
                stat(("k", j), 0, blk64)
            W2 = KVT * P
            blk = list(weights(("v", 0)))
            for c in range(NCH):
                start(("v", c))
                for k in range(KT):
                    b, o = blk[KVT * k]
                    ins = split_mm(gb(("v", c))[:, 0:W2], aH[:, k, c * P:(c + 1) * P], aL[:, k, c * P:(c + 1) * P],
                                   whi[b][:, o:o + W2], wlo[b][:, o:o + W2], k == 0, k == KT - 1)
                ins.then_inc(gemm_done, 1)
            feature_tile(("q", 0), in_a, in_a_lo)
            stat(("q", 0), 0, blk64)

            def scores_for_max(h, i):
                n = NCH * h + i
                if i == 0:
                    pe.wait_ge(q_ready, h + 1)
                    pe.wait_ge(k_ready, N_KV)
                    if h:
                        pe.wait_ge(row_ready, h)
                if n >= 2:
                    pe.wait_ge(mx_red, n - 1)
                mm(M[i % 2][:, :], qH[h % 4][0:HD, i * P:(i + 1) * P], kH[h // 4][0:HD, :], start=True,
                   stop=True).then_inc(mx_done, 1)

            def row_of_max(h):
                pe.wait_ge(mx_red, NCH * (h + 1))
                for i in range(NCH):
                    ins = nc.tensor.transpose(M[0][0:1, i * P:(i + 1) * P], mx[h % 2][:, i:i + 1], ident)
                ins.then_inc(rows_done, 1)

            def scores(h):
                g, b = h // 4, h % 4
                pe.wait_ge(row_ready, h + 1)
                pe.wait_ge(fills, 1)
                for c in range(NCH):
                    n = NCH * h + c
                    w = slice(c * P, (c + 1) * P)
                    if n >= 2:
                        pe.wait_ge(exp_done, n - 1)
                    split_mm(S[n % 2][:, :], kH[g][:, w], kL[g][:, w], qH[b][:, :], qL[b][:, :], True,
                             True).then_inc(qk_done, 1)

            def values(h, c):
                pe.wait_ge(exp_done, NCH * h + c + 1)
                if c == 0 and h:
                    pe.wait_ge(o_ev, h)
                mm(OP[:, :], vv[:, c, h // 4, :], PT[:, c, :], start=(c == 0), stop=(c == NCH - 1)).then_inc(pv_done, 1)

            pe.wait_ge(y_ev, PAIRS)
            for i in range(NCH):
                scores_for_max(0, i)
            row_of_max(0)
            for c in range(NCH):
                wait_evac(pe, ("v", c))
            for h in range(N_Q):
                u = h // 2
                scores(h)
                if h % 2 == 0 and u + 1 < QT:
                    feature_tile(("q", u + 1), in_a, in_a_lo)
                for c in range(NCH):
                    if h + 1 < N_Q:
                        scores_for_max(h + 1, c)
                    if c == NCH - 1 and h + 1 < N_Q:
                        row_of_max(h + 1)
                    values(h, c)
                if h % 2 == 0 and u + 1 < QT:
                    stat(("q", u + 1), 0, blk64)

            for m in range(KT):
                feature_tile(("ga", m), in_a, in_a_lo)
                feature_tile(("gs", m), in_a, in_a_lo)
                feature_tile(("wa", m), in_b, in_b_lo, (rdyB, PAIRS))
                if m == KT // 2:
                    pe.wait_ge(o_ev, N_Q)
                    ada_reduce(acc2, 1)
            ada_reduce(acc2, 2)
            for m in range(KT):
                feature_tile(("wo", m), lambda k: cH[:, k, :], lambda k: cL[:, k, :], (rdyC, 0))
                if m:
                    stat("n2", m - 1)
            stat("n2", KT - 1)

            for f in range(FQ):
                for m in range(KT):
                    feature_tile(("m1", f, m), in_a, in_a_lo, (rdyA, KT))
                for m in range(KT):
                    feature_tile(("m2", f, m), in_b, in_b_lo, (rdyB, 24 + KT * f))
                    if f == FQ - 1 and m:
                        stat("na", m - 1)
            stat("na", KT - 1)

            def gates(n):
                for w in ("rg", "ig"):
                    feature_tile((w, n), lambda k: xH[n % 2][:, :], lambda k: xL[n % 2][:, :], (rdyX, n))

            for n in range(RT):
                feature_tile(("xb", n), in_a, in_a_lo, (rdyA, 2 * KT))
                if n:
                    gates(n - 1)
            gates(RT - 1)
            for n in range(RT):
                feature_tile(("gt", n), in_a, in_a_lo)
            pe.wait_ge(rdyB, 24 + KT * FQ + KT)
            pe.wait_ge(rdyY, RT - KT)
            for m in range(KT):
                feature_tile(("oa", m), lambda k: bH[:, k, :] if k < KT else yH[:, k - KT, :],
                             lambda k: bL[:, k, :] if k < KT else yL[:, k - KT, :])
                if m:
                    stat("nkv", m - 1)
            stat("nkv", KT - 1)

            for i in range(CKT):
                feature_tile(("ck", i), in_a, in_a_lo, (rdyA, 3 * KT))
            feature_tile(("kr",), in_a, in_a_lo)
            for i in range(CKT):
                stat("ckv", i)
            for i in range(CQT):
                feature_tile(("cq", i), in_b, in_b_lo, (rdyB, 24 + KT * FQ + KT))
                stat("cq", i)

            def head_gemms1(h):
                feature_tile(("qr", h), lambda k: cqH[:, k, :], lambda k: cqL[:, k, :], (rdyK, CKT))
                feature_tile(("kn", h), lambda k: ckH[:, k, :], lambda k: ckL[:, k, :], (rdyK, 0))
                feature_tile(("qn", h), lambda k: cqH[:, k, :], lambda k: cqL[:, k, :])

            def head_values(h):
                name = ("vh", h)
                start(name)
                blk = list(weights(name))
                for c in range(NCH):
                    w = slice(c * P, (c + 1) * P)
                    for k, (b, o) in enumerate(blk):
                        ins = split_mm(gb(name)[:, w], ckH[:, k, w], ckL[:, k, w], whi[b][:, o:o + P],
                                       wlo[b][:, o:o + P], k == 0, k == CKT - 1)
                ins.then_inc(gemm_done, 1)

            def scores_for_max2(h, i):
                n = NCH * h + i
                b = h % 2
                if i == 0:
                    pe.wait_ge(kr_ready, 1)
                    wait_evac(pe, ("kn", h))
                    pe.wait_ge(qr_ready, h + 1)
                    wait_evac(pe, ("qn", h))
                    if h:
                        pe.wait_ge(row2, h)
                if n >= 2:
                    pe.wait_ge(mxr2, n - 1)
                w, keys = slice(i * P, (i + 1) * P), (i + 1) * P
                out = M[i % 2][:, 0:keys]
                mm(out, qnH[b][:, w], knH[b][:, 0:keys], start=True, stop=False)
                mm(out, qrH[b][0:QK_ROPE, w], krH[0:QK_ROPE, 0:keys], start=False, stop=False)
                mm(M[i % 2][:, w], identb, mask_qk, start=False, stop=True).then_inc(mxd2, 1)

            def row_of_max2(h):
                pe.wait_ge(mxr2, NCH * (h + 1))
                for i in range(NCH):
                    ins = nc.tensor.transpose(M[0][0:1, i * P:(i + 1) * P], mx[h % 2][:, i:i + 1], ident)
                ins.then_inc(rows2, 1)

            def scores2(h):
                b = h % 2
                pe.wait_ge(row2, h + 1)
                for c in range(NCH):
                    n = NCH * h + c
                    w, q = slice(c * P, (c + 1) * P), slice(c * P, SEQ)
                    if n >= 2:
                        pe.wait_ge(exp2, n - 1)
                    out = S[n % 2][:, q]
                    split_mm(out, knH[b][:, w], knL[b][:, w], qnH[b][:, q], qnL[b][:, q], True, False)
                    split_mm(out, krH[:, w], krL[:, w], qrH[b][:, q], qrL[b][:, q], False, False)
                    mm(S[n % 2][:, w], identb, mask_kq, start=False, stop=True).then_inc(qk2, 1)

            def values2(h, c):
                pe.wait_ge(exp2, NCH * h + c + 1)
                if c == 0 and h:
                    pe.wait_ge(o2, h)
                q = slice(c * P, SEQ)
                mm(OP[:, q], vm[h % 2][:, c, :], PT2[:, c, q], start=(c == 0), stop=(c == NCH - 1))
                mm(DEN[:, q], ones, PT2[:, c, q], start=(c == 0), stop=(c == NCH - 1)).then_inc(pv2, 1)

            head_gemms1(0)
            head_values(0)
            for i in range(NCH):
                scores_for_max2(0, i)
            feature_tile(("gh", 0), in_b, in_b_lo)
            row_of_max2(0)
            for h in range(N_HEADS):
                scores2(h)
                if h + 1 < N_HEADS:
                    head_gemms1(h + 1)
                wait_evac(pe, ("vh", h))
                for c in range(NCH):
                    values2(h, c)
                if h + 1 < N_HEADS:
                    head_values(h + 1)
                    for i in range(NCH):
                        scores_for_max2(h + 1, i)
                    feature_tile(("gh", h + 1), in_b, in_b_lo)
                    row_of_max2(h + 1)
            for m in range(KT):
                feature_tile(("ob", m), in_a, in_a_lo, (rdyA, 4 * KT))
                if m:
                    stat("fin", m - 1)
            stat("fin", KT - 1)

        @block.vector
        def _(ve):
            v = Steps(ve, v_step)
            V = nc.vector

            ve.wait_ge(s_in, 64)
            v(V.memset(eps, EPS))
            v(V.tensor_scalar(cwh, prm[:, PCOL["cw"][0]:PCOL["cw"][0] + 6 * 24], 0.5, None, ALU.mult))
            v(V.tensor_scalar(w05, col("ssdn", 0, PAIRS), 0.5, None, ALU.mult))
            V.tensor_scalar(hbr, prm[:, PCOL["brg"][0]:PCOL["brg"][0] + 2 * RT], 0.5, None, ALU.mult).then_inc(vec_prep, 1)
            V.scalar_tensor_tensor(lt[:, 0:RT], col("lam", 0, RT), -1.0, col("lam", 0, RT), ALU.mult, ALU.min)\
                .then_inc(lam_e, 1)
            ve.wait_ge(c_th, 1)
            v(V.tensor_scalar(csl, cth, 0.5, 0.5, ALU.mult, ALU.add))
            v.settle()
            v(V.tensor_tensor(csl, csl, col("c", 0, KT), ALU.mult))
            v.settle()

            def ada_add(p, pieces, into):
                k = p % KT
                ve.wait_ge(ada_in[p % 2], 16 * (p // 2 + 1))
                if k == 0:
                    if p:
                        ve.wait_ge(ada_red, p // KT)
                    V.tensor_scalar(into[:, :], pieces[p % 2][:, :], csl[:, 0:1], None, ALU.mult).then_inc(ada_acc, 1)
                else:
                    ve.wait_ge(ada_acc, p)
                    V.scalar_tensor_tensor(into[:, :], pieces[p % 2][:, :], csl[:, k:k + 1], into[:, :], ALU.mult,
                                           ALU.add).then_inc(ada_acc, 1)

            def ada_finish(j):
                ve.wait_ge(ada_red, j + 1)
                w = slice(2 * KT * j, 2 * KT * (j + 1))
                V.tensor_tensor(modc[:, w], ADA[:, 0:2 * KT], col("bada", 2 * KT * j, 2 * KT), ALU.add)\
                    .then_inc(mod_ready, 1)
                ve.wait_ge(mod_ready, j + 1)

            def inverse(norm):
                j = NORM_AT[norm]
                ve.wait_ge(std_ready, j + 1)
                V.reciprocal(rstd[:, :], std[:, :]).then_inc(rstd_ready, 1)
                ve.wait_ge(rstd_ready, j + 1)

            def norm_split(n0, gain, hi, lo, hi_sem, hi0, rdy, shift=None):
                def low(k):
                    ve.wait_ge(hi_sem, hi0 + k + 1)
                    if shift is None:
                        ins = V.tensor_tensor(lo[:, k, :], t[k % 2][:, :], r32(hi[:, k, :]), ALU.subtract)
                    else:
                        ins = V.scalar_tensor_tensor(lo[:, k, :], t[k % 2][:, :], shift(k), r32(hi[:, k, :]), ALU.add,
                                                     ALU.subtract)
                    ins.then_inc(rdy, 1)

                for k in range(KT):
                    if k >= 2:
                        low(k - 2)
                        ve.wait_ge(rdy, hi0 + k - 1)
                    V.scalar_tensor_tensor(t[k % 2][:, :], xF[:, k, :], gain(k), rstd[:, :], ALU.mult, ALU.mult)\
                        .then_inc(nfull, 1)
                low(KT - 2)
                low(KT - 1)
                ve.wait_ge(rdy, hi0 + KT)

            for p in range(KT):
                ada_add(p, piece, acc)
            ada_finish(0)
            v(V.scalar_tensor_tensor(gain1, modc[:, KT:2 * KT], 1.0, col("norm1", 0, KT), ALU.add, ALU.mult))
            v.settle()
            inverse("n1")
            norm_split(0, lambda k: gain1[:, k:k + 1], aH, aL, hiA, 0, rdyA, lambda k: modc[:, k:k + 1])

            def log1p(e, z, z2, p):
                v(V.tensor_scalar(p, e, 2.0, None, ALU.add))
                v.settle()
                v(V.reciprocal(p, p))
                v.settle()
                v(V.scalar_tensor_tensor(z, e, 2.0, p, ALU.mult, ALU.mult))
                v.settle()
                v(V.scalar_tensor_tensor(z2, z, 0.25, z, ALU.mult, ALU.mult))
                v.settle()
                v(V.tensor_scalar(p, z2, 1.0 / (2 * LOG_TERMS + 1), None, ALU.mult))
                v.settle()
                for k in range(LOG_TERMS - 1, 0, -1):
                    v(V.scalar_tensor_tensor(p, p, 1.0 / (2 * k + 1), z2, ALU.add, ALU.mult))
                    v.settle()
                v(V.scalar_tensor_tensor(p, p, 1.0, z, ALU.add, ALU.mult))
                v.settle()

            name = ("dt",)
            wait_tile(ve, name)
            psum = gb(name)[:, 0:NCH * R2].rearrange("p (c r) -> p c r", c=NCH)
            bias = tbc[:, None, 0:R2].broadcast_to([P, NCH, R2])
            inc_evac(V.tensor_tensor(dtT[:, :, :], psum, bias, ALU.add), name)
            wait_evac(ve, name)
            V.scalar_tensor_tensor(dtw[:, :, :], dtT[:, :, :], -1.0, dtT[:, :, :], ALU.mult, ALU.min).then_inc(sp_x, 1)
            ve.wait_ge(sp_e, 1)
            log1p(dtw[:, :, :], decB[:, :, :], dtx[:, :, :], wS[:, :, :])
            v(V.scalar_tensor_tensor(dtT[:, :, :], dtT[:, :, :], 0.0, wS[:, :, :], ALU.max, ALU.add))
            v.settle()
            ve.wait_ge(sp_e, 2)
            V.scalar_tensor_tensor(aT[:, :, :], dtT[:, :, :], -1.0, tbc[:, None, R2:2 * R2].broadcast_to([P, NCH, R2]),
                                   ALU.mult, ALU.mult).then_inc(a_ready, 1)
            ve.wait_ge(lam_l, 1)
            e, lp = lt[:, RT:2 * RT], lt[:, 2 * RT:3 * RT]
            log1p(e, lt[:, 3 * RT:4 * RT], lt[:, 0:RT], lp)
            v(V.scalar_tensor_tensor(e, col("lam", 0, RT), 0.0, lp, ALU.min, ALU.subtract))
            v.settle()
            V.tensor_scalar(nsp, e, 2.0, None, ALU.mult).then_inc(lam_e, 1)

            def conv(name):
                q = CONV_AT[name]
                i = {"xs": name[1], "B": 16 + name[1], "C": 20 + name[1]}[name[0]]
                out, src = t[q % 2], gb(name)
                ve.wait_ge(conv0, q + 1)
                for n, j in enumerate((0, 1, 3, 4)):
                    sh = j - 2
                    o = slice(max(0, -sh), SEQ - max(0, sh))
                    s = slice(max(0, sh), SEQ + min(0, sh))
                    ins = V.scalar_tensor_tensor(out[:, o], src[:, s], cwh[:, j * 24 + i:j * 24 + i + 1], out[:, o],
                                                 ALU.mult, ALU.add)
                    if n < 3:
                        v(ins)
                        v.settle()
                    else:
                        inc_evac(ins, name)
                dst = {"xs": xsF, "B": BF, "C": CF}[name[0]][name[1] % 2]
                ve.wait_ge(conv_th, q + 1)
                V.scalar_tensor_tensor(dst[:, :], t[2 + q % 2][:, :], 1.0, out[:, :], ALU.add, ALU.mult)\
                    .then_inc(conv_done, 1)

            def z_gate(i):
                name = ("z", i)
                ve.wait_ge(z_th, i + 1)
                inc_evac(V.scalar_tensor_tensor(zth[i % 2], zth[i % 2], 1.0, gb(name)[:, :], ALU.add, ALU.mult), name)

            conv(("B", 0))
            conv(("C", 0))
            ve.wait_ge(cs_done, 1)
            v(V.tensor_copy(csT[:, :, :], STB[:, 0:NCH * R2]))
            v.settle()
            ve.wait_ge(decb, 1)
            V.tensor_tensor(dtw[:, :, :], STF[:, 0:NCH * R2].rearrange("p (c r) -> p c r", c=NCH), csT[:, :, :],
                            ALU.subtract).then_inc(tot_e, 1)
            conv(("xs", 0))
            z_gate(0)
            ve.wait_ge(wdec, 1)
            v(V.tensor_tensor(wS[:, :, :], wS[:, :, :], dtT[:, :, :], ALU.mult))
            v.settle()

            def so_evac(g):
                for m in range(KT):
                    name = ("so", g, m)
                    wait_tile(ve, name)
                    if g == 0:
                        inc_evac(V.tensor_copy(xF[:, m, :], gb(name)[:, :]), name)
                    else:
                        inc_evac(V.tensor_tensor(xF[:, m, :], xF[:, m, :], gb(name)[:, :], ALU.add), name)

            for i in range(PAIRS):
                g, pg = i // PPG, i % PPG
                ve.wait_ge(xt_done, i + 1)
                if i:
                    ve.wait_ge(y_done, i)
                xt = XT[:, :].rearrange("p (c h d) -> p c h d", c=NCH, h=2)
                for n, (buf, tab, dd) in enumerate(((XS[0], wS, 0), (XS[1], wS, 1), (XS[2], dtT, 0), (XS[3], dtT, 1))):
                    h0 = dd * N_SSD + 2 * i
                    ins = V.tensor_tensor(buf[:, :, :].rearrange("p c (h d) -> p c h d", h=2), xt,
                                          tab[:, :, h0:h0 + 2, None].broadcast_to([P, NCH, 2, HD]), ALU.mult)
                ins.then_inc(xs_sc, 1)
                ve.wait_ge(csb_in, 16 * (i + 1))
                for r in range(4):
                    h = (r // 2) * N_SSD + 2 * i + r % 2
                    for c in range(NCH):
                        w = slice(c * P, (c + 1) * P)
                        ins = V.tensor_scalar(Dm[:, r, w], csB[:, r, w], csT[:, c, h:h + 1], 0.0, ALU.subtract, ALU.min)
                ins.then_inc(d_ready, 1)
                if pg == 0:
                    ve.wait_ge(cb_done, g + 1)
                    for buf, tri in zip(CB, (trif, trib)):
                        V.tensor_tensor(buf[:, :].rearrange("p (c l) -> p c l", c=NCH),
                                        STF[:, :].rearrange("p (c l) -> p c l", c=NCH),
                                        tri[:, None, :].broadcast_to([P, NCH, P]), ALU.mult).then_inc(cb_ev, 1)
                ve.wait_ge(e_ready, i + 1)
                V.tensor_tensor(Ex[:, :, :], Ex[:, :, :], CF[g % 2][:, None, :].broadcast_to([P, 4, SEQ]), ALU.mult)\
                    .then_inc(ce_ready, 1)
                if i + 1 < PAIRS:
                    if (i + 1) % PPG == 0:
                        conv(("B", g + 1))
                        conv(("C", g + 1))
                    conv(("xs", i + 1))
                ve.wait_ge(ed_ready, i + 1)
                ve.wait_ge(cb_ev, 2 * (g + 1))
                for dd in range(2):
                    V.tensor_tensor(Dm[:, 2 * dd:2 * dd + 2, :], Dm[:, 2 * dd:2 * dd + 2, :],
                                    CB[dd][:, None, :].broadcast_to([P, 2, SEQ]), ALU.mult).then_inc(m_ready, 1)
                ve.wait_ge(st_done, i + 1)
                v(V.tensor_copy(prev[:, 0, 0, :], STF[:, 0:P]))
                v(V.tensor_copy(prev[:, 1, 2, :], STB[:, 2 * P:3 * P]))
                for n in (1, 2):
                    v.settle()
                    for dd, slot, src in ((0, n, n - 1), (1, 2 - n, 3 - n)):
                        ps = (STF, STB)[dd]
                        c = n if dd == 0 else 3 - n
                        for hh in range(2):
                            hp = slice(hh * HD, (hh + 1) * HD)
                            h = dd * N_SSD + 2 * i + hh
                            st = ps[:, (c if dd == 0 else c - 1) * P + hh * HD:(c if dd == 0 else c - 1) * P + (hh + 1) * HD]
                            ins = V.scalar_tensor_tensor(prev[:, dd, slot, hp], prev[:, dd, src, hp],
                                                         decB[:, c, h:h + 1], st, ALU.mult, ALU.add)
                            if n == 2 and dd == 1 and hh == 1:
                                ins.then_inc(rec_done, 1)
                            else:
                                v(ins)
                if i + 1 < PAIRS:
                    z_gate(i + 1)
                ve.wait_ge(y_done, i + 1)
                wait_evac(ve, ("z", i))
                yz = t_yz[i % 2]
                V.scalar_tensor_tensor(yz, yz, col("ssdD", i), YP[:, :], ALU.mult, ALU.add).then_inc(y_ev, 1)
                ve.wait_ge(y_ev, i + 1)
                V.tensor_tensor(yz, yz, zth[i % 2], ALU.mult).then_inc(yz_ready, 1)
                ve.wait_ge(hiB, i + 1)
                ve.wait_ge(yz_ready, i + 1)
                V.scalar_tensor_tensor(bL[:, i % KT, :], yz, w05[:, i:i + 1], r32(bH[:, i % KT, :]), ALU.mult,
                                       ALU.subtract).then_inc(rdyB, 1)
                if pg == 0 and i:
                    so_evac(g - 1)
            so_evac(N_GROUPS - 1)
            ve.wait_ge(std_ready, NORM_AT["ssd"] + 1)
            V.reciprocal(rs_ssd[:, :], std[:, :]).then_inc(rstd_ready, 1)

            v(V.memset(vv[:, :, :, HD:P], 1.0))
            for g in range(N_KV):
                v(V.memset(r32(kH[g][HD:HD + 1, :]), 1.0))
                v(V.memset(r32(kL[g][HD:HD + 1, :]), 0.0))
            for b in range(4):
                ins = V.memset(r32(qL[b][HD:HD + 1, :]), 0.0)
                v(ins) if b < 3 else ins.then_inc(fills, 1)

            def rotate(name, j, outs, ready):
                wait_evac(ve, name)
                v(V.stream_shuffle(t[2][:, :], t[j % 2][:, :], SWAP))
                v(V.tensor_tensor(t[3][:, :], t[j % 2][:, :], rope1[:, 0, :], ALU.mult))
                v.settle()
                v(V.tensor_tensor(t[2][:, :], t[2][:, :], rope1[:, 1, :], ALU.mult))
                v.settle()
                V.tensor_tensor(t[3][:, :], t[3][:, :], t[2][:, :], ALU.add).then_inc(rope_done, 1)
                ve.wait_ge(rope_done, j + 1)
                inverse(name)
                for hh, (hi, lo) in enumerate(outs):
                    hp = slice(hh * HD, (hh + 1) * HD)
                    v(V.tensor_tensor(t[2][0:HD, :], t[3][hp, :], rstd[hp, :], ALU.mult))
                    v.settle()
                    v(V.tensor_copy(hi[0:HD, :], t[2][0:HD, :]))
                    v.settle()
                    V.tensor_tensor(lo[0:HD, :], t[2][0:HD, :], r32(hi[0:HD, :]), ALU.subtract).then_inc(ready, 1)
                    ve.wait_ge(ready, (2 * j if ready is k_ready else 2 * (j - KVT)) + hh + 1)

            ve.wait_ge(s_rope, 16)
            for j in range(KVT):
                rotate(("k", j), j, [(kH[2 * j], kL[2 * j]), (kH[2 * j + 1], kL[2 * j + 1])], k_ready)
            rotate(("q", 0), KVT, [(qH[0], qL[0]), (qH[1], qL[1])], q_ready)

            def max_of(h, i):
                ve.wait_ge(mx_done, NCH * h + i + 1)
                if i == 0 and h >= 2:
                    ve.wait_ge(rows_done, h - 1)
                V.tensor_reduce(mx[h % 2][:, i:i + 1], M[i % 2][:, :], AX, ALU.max).then_inc(mx_red, 1)

            for i in range(NCH):
                max_of(0, i)
            for h in range(N_Q):
                u = h // 2
                if h + 1 < N_Q:
                    for i in range(NCH):
                        max_of(h + 1, i)
                ve.wait_ge(pv_done, NCH * (h + 1))
                rd = t[2][0:HD, :]
                v(V.reciprocal(rd, OP[HD:P, :]))
                v.settle()
                at = t[4 + u % 2]
                V.tensor_tensor(at[h % 2 * HD:(h % 2 + 1) * HD, :], OP[0:HD, :], rd, ALU.mult).then_inc(o_ev, 1)
                if h % 2 == 0 and u + 1 < QT:
                    b = 2 * ((u + 1) % 2)
                    if u:
                        ve.wait_ge(qk_done, NCH * 2 * u)
                    ve.wait_ge(o_ev, h + 1)
                    rotate(("q", u + 1), KVT + u + 1, [(qH[b], qL[b]), (qH[b + 1], qL[b + 1])], q_ready)
                if h % 2:
                    ve.wait_ge(hiB, PAIRS + u + 1)
                    ve.wait_ge(o_ev, h + 1)
                    V.tensor_tensor(bL[:, u, :], at[:, :], r32(bH[:, u, :]), ALU.subtract).then_inc(rdyB, 1)

            for m in range(KT):
                out = t[4 + m % 2]
                wait_evac(ve, ("gs", m))
                v(V.scalar_tensor_tensor(xF[:, m, :], t[2 + m % 2][:, :], 1.0, xF[:, m, :], ALU.add, ALU.mult))
                v.settle()
                v(V.tensor_tensor(xF[:, m, :], xF[:, m, :], rs_ssd[:, :], ALU.mult))
                if m >= 2:
                    ve.wait_ge(hiC, m - 1)
                wait_tile(ve, ("wa", m))
                wait_evac(ve, ("ga", m))
                inc_evac(V.scalar_tensor_tensor(out[:, :], t[m % 2][:, :], 1.0, gb(("wa", m))[:, :], ALU.add, ALU.mult),
                         ("wa", m))
                wait_evac(ve, ("wa", m))
                v.settle()
                V.tensor_tensor(out[:, :], out[:, :], xF[:, m, :], ALU.add).then_inc(mrg, 1)
                ve.wait_ge(hiC, m + 1)
                ve.wait_ge(mrg, m + 1)
                V.scalar_tensor_tensor(cL[:, m, :], out[:, :], 0.5, r32(cH[:, m, :]), ALU.mult, ALU.subtract)\
                    .then_inc(rdyC, 1)
                if m == KT // 2:
                    ada_finish(1)
                for p in (KT + 2 * m, KT + 2 * m + 1):
                    ada_add(p, piece2, acc2)
            ada_finish(2)
            v(V.scalar_tensor_tensor(gain2, modc[:, 4 * KT:5 * KT], 1.0, col("norm2", 0, KT), ALU.add, ALU.mult))
            v.settle()
            ve.wait_ge(s_x2, 16)
            for m in range(KT):
                name = ("wo", m)
                wait_tile(ve, name)
                inc_evac(V.scalar_tensor_tensor(xF[:, m, :], gb(name)[:, :], modc[:, 2 * KT + m:2 * KT + m + 1],
                                                xF[:, m, :], ALU.mult, ALU.add), name)
            inverse("n2")
            norm_split(KT, lambda k: gain2[:, k:k + 1], aH, aL, hiA, KT, rdyA,
                       lambda k: modc[:, 3 * KT + k:3 * KT + k + 1])

            for f in range(FQ):
                for m in range(KT):
                    n = KT * f + m
                    wait_evac(ve, ("m1", f, m))
                    r, full = t[2 + n % 2], t[4 + n % 2]
                    v(V.tensor_tensor(full[:, :], r[:, :], r[:, :], ALU.mult))
                    v.settle()
                    ve.wait_ge(hiB, 24 + n + 1)
                    V.tensor_tensor(bL[:, m, :], full[:, :], r32(bH[:, m, :]), ALU.subtract).then_inc(rdyB, 1)
                for m in range(KT):
                    name = ("m2", f, m)
                    wait_tile(ve, name)
                    inc_evac(V.scalar_tensor_tensor(xF[:, m, :], gb(name)[:, :], modc[:, 5 * KT + m:5 * KT + m + 1],
                                                    xF[:, m, :], ALU.mult, ALU.add), name)

            inverse("na")
            norm_split(2 * KT, lambda k: col("na", k), aH, aL, hiA, 2 * KT, rdyA)

            def conv_rnn(n):
                name, out = ("xb", n), xacc[n % 2]
                ve.wait_ge(c20, n + 1)
                for j in range(3):
                    sh = 3 - j
                    ins = V.scalar_tensor_tensor(out[:, sh:SEQ], gb(name)[:, 0:SEQ - sh], col("cw2", j * RT + n),
                                                 out[:, sh:SEQ], ALU.mult, ALU.add)
                    if j < 2:
                        v(ins)
                        v.settle()
                    else:
                        inc_evac(ins, name)
                ve.wait_ge(hiX, n + 1)
                wait_evac(ve, name)
                V.tensor_tensor(xL[n % 2][:, :], out[:, :], r32(xH[n % 2][:, :]), ALU.subtract).then_inc(rdyX, 1)

            def gate_x(n):
                wait_evac(ve, ("ig", n))
                V.scalar_tensor_tensor(xbi[:, n, :], t[4 + n % 2][:, :], 1.0, xacc[n % 2][:, :], ALU.add, ALU.mult)\
                    .then_inc(xbi_done, 1)

            for n in range(RT):
                conv_rnn(n)
                if n:
                    gate_x(n - 1)
            gate_x(RT - 1)
            ve.wait_ge(xbi_done, RT)
            for n in range(RT):
                ve.wait_ge(s_done, n + 1)
                V.tensor_tensor(xbi[:, n, :], xbi[:, n, :], t[2 + n % 2][:, :], ALU.mult).then_inc(xbs_done, 1)
            ve.wait_ge(xbs_done, RT)
            for n in range(RT):
                name, th = ("gt", n), t[4 + n % 2]
                q = xacc[0]
                v(V.tensor_scalar(q[:, :], t2[:, n, :], -1.0, 1.0, ALU.mult, ALU.add))
                v.settle()
                v(V.reciprocal(q[:, :], q[:, :]))
                v.settle()
                v(V.scalar_tensor_tensor(t2[:, n, :], t2[:, n, :], 1.0, q[:, :], ALU.add, ALU.mult))
                v(V.tensor_tensor(xbi[:, n, :], xbi[:, n, :], q[:, :], ALU.mult))
                v.settle()
                v(V.tensor_tensor_scan(xacc[1][:, :], t2[:, n, :], xbi[:, n, :], 0.0, ALU.mult, ALU.add))
                ve.wait_ge(g_th, n + 1)
                inc_evac(V.scalar_tensor_tensor(th[:, :], th[:, :], 1.0, gb(name)[:, :], ALU.add, ALU.mult), name)
                wait_evac(ve, name)
                v.settle()
                V.tensor_tensor(t[n % 2][:, :], xacc[1][:, :], th[:, :], ALU.mult).then_inc(y2_ready, 1)
                if n < KT:
                    ve.wait_ge(hiB, 24 + KT * FQ + n + 1)
                    hi, lo, rdy = bH[:, n, :], bL[:, n, :], rdyB
                else:
                    ve.wait_ge(hiY, n - KT + 1)
                    hi, lo, rdy = yH[:, n - KT, :], yL[:, n - KT, :], rdyY
                V.scalar_tensor_tensor(lo, t[n % 2][:, :], 0.5, r32(hi), ALU.mult, ALU.subtract).then_inc(rdy, 1)

            def add_to_stream(name, m):
                wait_tile(ve, name)
                inc_evac(V.tensor_tensor(xF[:, m, :], xF[:, m, :], gb(name)[:, :], ALU.add), name)

            for m in range(KT):
                add_to_stream(("oa", m), m)

            inverse("nkv")
            norm_split(3 * KT, lambda k: col("nkv", k), aH, aL, hiA, 3 * KT, rdyA)
            norm_split(4 * KT, lambda k: col("nb", k), bH, bL, hiB, 24 + KT * FQ + KT, rdyB)

            v(V.memset(r32(krH[QK_ROPE:QK_ROPE + 1, :]), 1.0))
            v(V.memset(r32(krL[QK_ROPE:QK_ROPE + 1, :]), 0.0))
            for b in range(2):
                v(V.memset(r32(qrL[b][QK_ROPE:QK_ROPE + 1, :]), 0.0))

            def compress(norm, gain, n0, tiles, lo):
                def low(i):
                    ve.wait_ge(hiK, n0 + i + 1)
                    hi = (ckH if lo is ckL else cqH)[:, i, :]
                    V.tensor_tensor(lo[:, i, :], t[i % 2][:, :], r32(hi), ALU.subtract).then_inc(rdyK, 1)

                inverse(norm)
                for i in range(tiles):
                    if i >= 2:
                        low(i - 2)
                        ve.wait_ge(rdyK, n0 + i - 1)
                    V.scalar_tensor_tensor(t[i % 2][:, :], ckf[:, i, :], col(gain, i), rstd[:, :], ALU.mult, ALU.mult)\
                        .then_inc(ck_x, 1)
                for i in range(max(0, tiles - 2), tiles):
                    low(i)

            def rope(name, hi, lo, ready):
                wait_tile(ve, name)
                R = QK_ROPE
                v(V.tensor_tensor(t[0][0:R, :], gb(name)[0:R, :], rope2[0:R, :], ALU.mult))
                inc_evac(V.tensor_tensor(t[1][0:R, :], gb(name)[R:P, :], rope2[R:P, :], ALU.mult), name)
                wait_evac(ve, name)
                v.settle()
                v(V.tensor_tensor(t[0][0:R, :], t[0][0:R, :], t[1][0:R, :], ALU.add))
                v.settle()
                v(V.tensor_copy(hi[0:R, :], t[0][0:R, :]))
                v.settle()
                V.tensor_tensor(lo[0:R, :], t[0][0:R, :], r32(hi[0:R, :]), ALU.subtract).then_inc(ready, 1)

            compress("ckv", "kvn", 0, CKT, ckL)
            ve.wait_ge(rope2_in, 16)
            ve.wait_ge(rdyK, CKT)
            rope(("kr",), krH, krL, kr_ready)
            compress("cq", "qn2", CKT, CQT, cqL)

            def head_low(h):
                b = h % 2
                rope(("qr", h), qrH[b], qrL[b], qr_ready)
                for n, hi, lo, done in (("kn", knH, knL, kn_hi), ("qn", qnH, qnL, qn_hi)):
                    ve.wait_ge(done, h + 1)
                    inc_evac(V.tensor_tensor(lo[b][:, :], gb((n, h))[:, :], r32(hi[b][:, :]), ALU.subtract), (n, h))

            def max_and_gate(h):
                for i in range(NCH):
                    ve.wait_ge(mxd2, NCH * h + i + 1)
                    if i == 0 and h >= 2:
                        ve.wait_ge(rows2, h - 1)
                    V.tensor_reduce(mx[h % 2][:, i:i + 1], M[i % 2][:, 0:(i + 1) * P], AX, ALU.max).then_inc(mxr2, 1)
                ve.wait_ge(gh_th, h + 1)
                inc_evac(V.scalar_tensor_tensor(t[4 + h % 2][:, :], t[4 + h % 2][:, :], 1.0, gb(("gh", h))[:, :], ALU.add,
                                                ALU.mult), ("gh", h))

            head_low(0)
            max_and_gate(0)
            for h in range(N_HEADS):
                if h + 1 < N_HEADS:
                    head_low(h + 1)
                ve.wait_ge(pv2, NCH * (h + 1))
                v(V.reciprocal(t[3][:, :], DEN[:, :]))
                v.settle()
                V.tensor_tensor(t[3][:, :], OP[:, :], t[3][:, :], ALU.mult).then_inc(o2, 1)
                ve.wait_ge(o2, h + 1)
                wait_evac(ve, ("gh", h))
                V.tensor_tensor(t[2][:, :], t[3][:, :], t[4 + h % 2][:, :], ALU.mult).then_inc(yb, 1)
                if h + 1 < N_HEADS:
                    max_and_gate(h + 1)
                ve.wait_ge(hiA, 4 * KT + h + 1)
                ve.wait_ge(yb, h + 1)
                V.scalar_tensor_tensor(aL[:, h, :], t[2][:, :], 0.5, r32(aH[:, h, :]), ALU.mult, ALU.subtract)\
                    .then_inc(rdyA, 1)
            for m in range(KT):
                add_to_stream(("ob", m), m)
            inverse("fin")
            for m in range(KT):
                V.scalar_tensor_tensor(xF[:, m, :], xF[:, m, :], col("fin", m), rstd[:, :], ALU.mult, ALU.mult)\
                    .then_inc(fin_ready, 1)


def kernel(x, c, w_ada, b_ada, norm1_w, norm2_w, w_in, q_norm_w, k_norm_w, conv_w, conv_b, A_log, dt_bias, ssd_D,
           ssd_norm_w, w_attn_out, w_ssd_out, w_o, w_mlp1, w_mlp2, norm_a_2, w_in_a_2, conv_w_2, conv_b_2, w_rg_2,
           b_rg_2, w_ig_2, b_ig_2, lru_lambda_2, w_out_a_2, norm_kv_2, w_dkv_2, kv_norm_2, w_uk_2, w_uv_2, norm_b_2,
           w_in_b_2, q_norm_2, w_uq_2, w_out_b_2, final_norm_2):
    import ml_dtypes
    import numpy as np
    import concourse.bacc as bacc
    from concourse.bass_utils import run_bass_kernel_spmd

    f32 = np.float32

    def arr(a):
        return np.asarray(a, f32)

    w_in, w_in_b, w_in_a = arr(w_in)[0], arr(w_in_b_2)[0], arr(w_in_a_2)[0]
    w_so, w_wa, w_wo = arr(w_ssd_out)[0], arr(w_attn_out)[0], arr(w_o)[0]
    w_m1, w_m2, w_oa, w_ob = arr(w_mlp1)[0], arr(w_mlp2)[0], arr(w_out_a_2)[0], arr(w_out_b_2)[0]
    w_rg, w_ig, w_dkv = arr(w_rg_2)[0], arr(w_ig_2)[0], arr(w_dkv_2)
    w_uk, w_uv, w_uq = arr(w_uk_2), arr(w_uv_2), arr(w_uq_2)[0]
    HR = QK_ROPE // 2

    o_k = N_Q * HD
    o_v = o_k + N_KV * HD
    o_xs = o_v + N_KV * HD
    o_B = o_xs + D_INNER
    o_C = o_B + N_GROUPS * D_STATE
    o_z = o_C + N_GROUPS * D_STATE
    o_dt = o_z + D_INNER
    o_ga = o_dt + 2 * N_SSD
    o_gs = o_ga + D_MODEL

    def cols(w, a, i=0, n=P):
        return w[:, a + n * i:a + n * (i + 1)]

    def with_swapped_halves(w):
        return np.concatenate([w, w[:, HR:], w[:, :HR]], axis=1)

    def matrix(name):
        kind, i = name[0], name[1] if len(name) > 1 else 0
        return {
            "dt": lambda: cols(w_in, o_dt, 0, 2 * N_SSD), "B": lambda: cols(w_in, o_B, i),
            "C": lambda: cols(w_in, o_C, i), "xs": lambda: cols(w_in, o_xs, i), "z": lambda: cols(w_in, o_z, i),
            "so": lambda: cols(w_so[PPG * P * i:PPG * P * (i + 1)], 0, name[2]),
            "k": lambda: cols(w_in, o_k, i), "v": lambda: cols(w_in, o_v, 0, N_KV * HD), "q": lambda: cols(w_in, 0, i),
            "ga": lambda: cols(w_in, o_ga, i), "gs": lambda: cols(w_in, o_gs, i), "wa": lambda: cols(w_wa, 0, i),
            "wo": lambda: cols(w_wo, 0, i), "m1": lambda: cols(w_m1, D_MODEL * i, name[2]),
            "m2": lambda: cols(w_m2[D_MODEL * i:D_MODEL * (i + 1)], 0, name[2]),
            "xb": lambda: cols(w_in_a, 0, i), "gt": lambda: cols(w_in_a, D_RNN, i), "rg": lambda: w_rg[i],
            "ig": lambda: w_ig[i], "oa": lambda: cols(w_oa, 0, i), "ck": lambda: cols(w_dkv, 0, i),
            "kr": lambda: with_swapped_halves(w_dkv[:, KV_RANK:]), "cq": lambda: cols(w_in_b, 0, i),
            "qr": lambda: with_swapped_halves(w_uq[:, i, QK_NOPE:]), "kn": lambda: w_uk[:, i],
            "qn": lambda: w_uq[:, i, :QK_NOPE], "vh": lambda: w_uv[:, i], "gh": lambda: cols(w_in_b, Q_RANK, i),
            "ob": lambda: cols(w_ob, 0, i)}[kind]()

    stream = np.zeros((P, N_SLABS * SLAB), f32)
    at = 0
    for name, blocks in ORDER:
        if name != "pad":
            w = matrix(name)
            stream[:, at:at + blocks * P] = w.reshape(-1, P, w.shape[1]).transpose(1, 0, 2).reshape(P, -1)
        at += blocks * P
    stream = np.ascontiguousarray(stream.reshape(P, N_SLABS, SLAB).transpose(1, 0, 2))

    def feat(a):
        return arr(a).reshape(-1, P).T

    vectors = {
        "norm1": feat(norm1_w), "norm2": feat(norm2_w), "qn": feat(np.tile(arr(q_norm_w).ravel(), P // HD)),
        "kn": feat(np.tile(arr(k_norm_w).ravel(), P // HD)), "cw": feat(conv_w), "cb": feat(conv_b),
        "ssdD": feat(np.repeat(arr(ssd_D).ravel(), HD)), "ssdn": feat(ssd_norm_w), "na": feat(norm_a_2),
        "cw2": feat(conv_w_2), "cb2": feat(conv_b_2), "brg": feat(b_rg_2), "big": feat(b_ig_2),
        "lam": feat(lru_lambda_2), "nkv": feat(norm_kv_2), "kvn": feat(kv_norm_2), "nb": feat(norm_b_2),
        "qn2": feat(q_norm_2), "fin": feat(final_norm_2), "bada": feat(b_ada), "c": feat(c)}
    prm = np.ascontiguousarray(np.concatenate([vectors[n] for n, _ in _PRM], axis=1))

    r, s = np.arange(P)[:, None], np.arange(P)[None, :]
    blk = (r // HD == s // HD) / HD
    cst = np.concatenate([r == s, r <= s, r >= s, np.ones((P, P)), blk], axis=1).astype(f32)
    cstb = np.concatenate([r == s, np.where(s >= r, 0.0, -1e30), np.where(s <= r, 0.0, -1e30)], axis=1)
    cstb = cstb.astype(ml_dtypes.bfloat16)
    tok = np.arange(SEQ, dtype=f32)
    dim = np.arange(P) % HD
    half = HD // 2
    freq = 10000.0 ** (-2.0 * (dim % half % (half // 2)) / half)
    pos = np.where((dim < half)[:, None], tok[None] // 64, tok[None] % 64)
    ang = (pos.astype(f32) * freq[:, None].astype(f32)).astype(np.float64)
    sign = np.where(dim % half < half // 2, -1.0, 1.0)[:, None]
    rope1 = np.ascontiguousarray(np.stack([np.cos(ang), sign * np.sin(ang)], axis=1).astype(f32))
    dim = np.arange(QK_ROPE)
    freq = 10000.0 ** (-2.0 * (dim % HR) / QK_ROPE)
    ang = (tok[None] * freq[:, None].astype(f32)).astype(f32).astype(np.float64)
    sign = np.where(dim < HR, -1.0, 1.0)[:, None]
    rope2 = np.concatenate([np.cos(ang), sign * np.sin(ang)], axis=0).astype(f32)

    inputs = {
        "prm": prm, "cst": cst, "cstb": cstb, "ws": stream, "rope1": rope1, "rope2": rope2,
        "tb": np.ascontiguousarray(np.concatenate([arr(dt_bias).ravel(), arr(A_log).ravel()])),
        "ada": np.ascontiguousarray(arr(w_ada)[0].reshape(KT, P, ADA_G, ADA_W).transpose(2, 0, 1, 3)
                                    .reshape(ADA_G * KT, P, ADA_W)),
        "x": np.ascontiguousarray(arr(x)[0].T.reshape(KT, P, SEQ).transpose(1, 0, 2))}

    nc = bacc.Bacc("TRN2", target_bir_lowering=False, num_devices=1)
    d = {n: nc.dram_tensor(n, a.shape, BF16 if a.dtype != f32 else F32, kind="ExternalInput").ap()
         for n, a in inputs.items()}
    d["cs"] = nc.dram_tensor("cs_scratch", (2 * N_SSD, SEQ), F32, kind="Internal").ap()
    d["out"] = nc.dram_tensor("out", (KT, P, SEQ), F32, kind="ExternalOutput").ap()
    build(nc, d)
    res = run_bass_kernel_spmd(nc, [inputs], core_ids=[0])
    out = np.asarray(res.results[0]["out"]).reshape(D_MODEL, SEQ)
    return np.ascontiguousarray(out.T)[None]
```

```python
from contextlib import ExitStack

import concourse.bass as bass
from concourse import mybir

F32 = mybir.dt.float32
F32R = mybir.dt.float32r
BF16 = mybir.dt.bfloat16
ALU = mybir.AluOpType
ACT = mybir.ActivationFunctionType
AX = mybir.AxisListType.X

P = 128
D_MODEL, SEQ = 1024, 512
N_Q, N_KV, HD = 16, 4, 64
D_INNER, N_GROUPS, D_STATE, N_SSD = 2048, 4, 128, 32
D_FF = 4096
D_RNN, RNN_BLOCKS = 1280, 10
N_HEADS, QK_NOPE, QK_ROPE, V_DIM, KV_RANK, Q_RANK = 8, 128, 64, 128, 256, 384
EPS = 1e-6
LRU_C = 8.0
LOG_TERMS = 8

KT = D_MODEL // P
NCH = SEQ // P
PAIRS = D_INNER // P
PPG = PAIRS // N_GROUPS
QT = N_Q * HD // P
Q_RING = 6
KVT = N_KV * HD // P
FQ = D_FF // D_MODEL
RT = D_RNN // P
RNN_LAG = 2
XB = RNN_LAG + 1
CKT, CQT = KV_RANK // P, Q_RANK // P
BPS = 8
SLAB = BPS * P
RING = 3
AHEAD = 2

_PRM = [("norm1", KT), ("norm2", KT), ("qn", 1), ("kn", 1), ("cw", 5 * 24), ("cb", 24), ("ssdD", PAIRS),
        ("ssdn", PAIRS), ("na", KT), ("cw2", 4 * RT), ("cb2", RT), ("brg", RT), ("big", RT), ("lam", RT),
        ("nkv", KT), ("kvn", CKT), ("nb", KT), ("qn2", CQT), ("fin", KT), ("bada", 6 * KT), ("c", KT)]
PCOL, _n = {}, 0
for _name, _w in _PRM:
    PCOL[_name] = (_n, _w)
    _n += _w
N_PRM = _n
CONV_TILES = 24


QK = [(kind, t) for t in range(QT) for kind in ("k", "q") if kind == "q" or t < KVT]
QK_AT = {name: j for j, name in enumerate(QK)}


def between(i):
    g, pg = i // PPG, i % PPG
    names = []
    if i + 1 < PAIRS:
        names.append(("xs", i + 1))
    if g + 1 < N_GROUPS and pg >= 2:
        names.append(("B" if pg == 2 else "C", g + 1))
    if g:
        names += [("so", g - 1, m) for m in range(pg * KT // PPG, (pg + 1) * KT // PPG)]
    if i + 1 < PAIRS:
        names.append(("z", i + 1))
    return names


def plan():
    order, tiles, at = [], {}, 0

    def tile(name, blocks, advance=True):
        nonlocal at
        tiles[name] = (len(tiles), at, blocks)
        if advance:
            at += blocks
            order.append((name, blocks))

    tile(("B", 0), KT)
    tile(("C", 0), KT)
    tile(("dt",), KT // 2)
    order.append(("pad", BPS - KT // 2))
    at += BPS - KT // 2
    tile(("xs", 0), KT)
    tile(("z", 0), KT)
    for i in range(PAIRS):
        for name in between(i):
            tile(name, PPG if name[0] == "so" else KT)
    for m in range(KT):
        tile(("so", N_GROUPS - 1, m), PPG)
    for name in QK[:KVT + 1]:
        tile(name, KT)
    for c in range(NCH):
        tile(("v", c), KT * KVT, advance=(c == NCH - 1))
    for name in QK[KVT + 1:]:
        tile(name, KT)
    for m in range(KT):
        for w in ("ga", "gs", "wa"):
            tile((w, m), KT)
    for m in range(KT):
        tile(("wo", m), KT)
    for f in range(FQ):
        for m in range(KT):
            tile(("m1", f, m), KT)
        for m in range(KT):
            tile(("m2", f, m), KT)
    for n in range(RT + RNN_LAG):
        if n < RT:
            tile(("xb", n), KT)
        if n >= RNN_LAG:
            tile(("rg", n - RNN_LAG), 1)
            tile(("ig", n - RNN_LAG), 1)
    for n in range(RT):
        tile(("gt", n), KT)
    for m in range(KT):
        tile(("oa", m), RT)
    for t in range(CKT):
        tile(("ck", t), KT)
    tile(("kr",), KT)
    for t in range(CQT):
        tile(("cq", t), KT)
    for h in range(N_HEADS):
        tile(("qr", h), CQT)
        tile(("kn", h), CKT)
        tile(("qn", h), CQT)
        tile(("vh", h), CKT)
        tile(("gh", h), KT)
    for m in range(KT):
        tile(("ob", m), KT)
    if at % BPS:
        order.append(("pad", BPS - at % BPS))
        at += BPS - at % BPS
    return tiles, order, at // BPS


TILES, ORDER, N_SLABS = plan()
MIXER = ("dt", "B", "C", "xs", "z", "so")
NARROW = ("k", "v", "q", "qr", "kn", "qn", "vh", "gh")
BANK_OF, _used, _turn = {}, [0] * 8, 0
for _name in TILES:
    _ring = (0, 1, 7) if _name[0] in MIXER else (0, 1) if _name[0] in NARROW else (0, 1, 3, 4, 5, 6)
    _b = _ring[_turn % len(_ring)]
    BANK_OF[_name] = (_b, _used[_b])
    _used[_b] += 1
    _turn += 1
CONV = [n for n in TILES if n[0] in ("B", "C", "xs")]
CONV_AT = {n: q for q, n in enumerate(CONV)}
NORMS = ([("n1", KT), ("ssd", PAIRS)] + [(name, 1) for name in QK] + [("n2", KT), ("na", KT), ("nkv", KT), ("ckv", CKT), ("cq", CQT), ("fin", KT)])
NORM_AT, STAT_AT, _n = {}, {}, 0
for _j, (_name, _w) in enumerate(NORMS):
    NORM_AT[_name], STAT_AT[_name] = _j, (_n, _w)
    _n += _w
POOLED = ("ssd", "n2", "na", "nkv", "fin")
POOL_AT, SUM_AT, SQ_USED, _p, _s = {}, {}, [], 0, 0
for _name, _w in NORMS:
    POOL_AT[_name] = _p
    for _k in range(_w):
        if _name in POOLED and _k < _w - 1:
            _p += _k > 0
            SQ_USED.append(("pool", max(_p, POOL_AT[_name] + 1)))
        else:
            _s += 1
            SQ_USED.append(("pe", _s))
    SUM_AT[_name] = _s
ADA_W = 2 * D_MODEL
ADA_G = 3
ADA_RING = 5
SWAP = [i ^ 16 for i in range(32)]


def slab_of(name):
    return TILES[name][1] // BPS


LAST_TILE = {}
for _name in TILES:
    _, _at, _b = TILES[_name]
    for _s in range(_at // BPS, (_at + _b - 1) // BPS + 1):
        LAST_TILE[_s] = TILES[_name][0]


class Steps:

    def __init__(self, eng, sem):
        self.eng, self.sem, self.n = eng, sem, 0

    def __call__(self, ins):
        ins.then_inc(self.sem, 1)
        self.n += 1

    def settle(self):
        self.eng.wait_ge(self.sem, self.n)


def build(nc, d):
    with ExitStack() as ctx:
        stack = [ctx]

        def sb(name, shape, dt=F32):
            return stack[-1].enter_context(nc.sbuf_tensor(name, shape, dt))

        def sem(name):
            return ctx.enter_context(nc.semaphore(name))

        class Arena:

            def __enter__(self):
                stack.append(ExitStack())
                return self

            def __exit__(self, *e):
                stack.pop().close()

        raw = [sb(f"w_raw{b}", [P, SLAB]) for b in range(RING)]
        whi = [sb(f"w_hi{b}", [P, SLAB], F32R) for b in range(RING)]
        wlo = [sb(f"w_lo{b}", [P, SLAB], F32R) for b in range(RING)]
        xF = sb("x_stream", [P, KT, SEQ])
        aH, aL = sb("a_hi", [P, KT, SEQ], F32R), sb("a_lo", [P, KT, SEQ], F32R)
        bH, bL = sb("b_hi", [P, KT, SEQ], F32R), sb("b_lo", [P, KT, SEQ], F32R)
        prm = sb("params", [P, N_PRM])
        cst = sb("consts", [P, 5 * P])
        cstb = sb("consts_bf16", [P, 3 * P], BF16)
        tbc = sb("dt_bias_and_A_log", [P, 4 * N_SSD])
        small = sb("small", [P, 320])
        t = [sb(f"tmp{i}", [P, SEQ]) for i in range(6)]
        sq = [sb(f"sq{i}", [P, SEQ]) for i in range(2)]
        sq_sum = sb("square_sum", [P, SEQ])
        std, rstd, rs_ssd = sb("std", [P, SEQ]), sb("rstd", [P, SEQ]), sb("rstd_ssd", [P, SEQ])

        ident, trif, trib, ones, blk64 = (cst[:, i * P:(i + 1) * P] for i in range(5))
        identb, mask_kq, mask_qk = (cstb[:, i * P:(i + 1) * P] for i in range(3))

        def col(name, i=0, n=1):
            a = PCOL[name][0] + i
            return prm[:, a:a + n]

        modc, gain1, gain2 = small[:, 0:48], small[:, 48:56], small[:, 56:64]
        csl, cth, eps = small[:, 64:72], small[:, 72:80], small[:, 80:81]
        w05, cwh, hbr = small[:, 82:98], small[:, 98:242], small[:, 242:262]
        nsp, lt = small[:, 262:272], small[:, 272:312]
        nsp2 = lt[:, 0:RT]
        mx = [small[:, 312:316], small[:, 316:320]]

        with Arena():
            piece = [sb(f"ada_piece{b}", [P, ADA_W]) for b in range(ADA_RING)]
            acc = sb("ada_acc", [P, ADA_W])
        with Arena():
            csB = sb("cs_rows", [P, 4, SEQ])
            Ex = sb("C_decayed", [P, 4, SEQ])
            Dm = sb("M", [P, 4, SEQ])
            XS = [sb(n, [P, NCH, P]) for n in ("X_state_f", "X_state_b", "X_f", "X_b")]
            BF = [sb(f"B_feat{b}", [P, SEQ]) for b in range(2)]
            CF = [sb(f"C_feat{b}", [P, SEQ]) for b in range(2)]
            BT = sb("B_tok", [P, NCH, P])
            CB = [sb(n, [P, SEQ]) for n in ("CB_f", "CB_b")]
            prev = sb("states", [P, 2, 3, P])
            xsF = [sb(f"x_feat{b}", [P, SEQ]) for b in range(2)]
            R2 = 2 * N_SSD
            dtT, csT, aT, wS, decB, dtw = (sb(n, [P, NCH, R2]) for n in ("dt", "cs", "a", "dt_decay", "chunk_decay",
                                                                          "dt_work"))
            dtx = sb("dt_work2", [P, NCH, R2])
            csF = Dm[0:R2, 0, :]
        with Arena():
            rope1 = sb("rope1_table", [P, 2, SEQ])
            kH = [sb(f"k_hi{g}", [HD + 1, SEQ], F32R) for g in range(N_KV)]
            kL = [sb(f"k_lo{g}", [HD + 1, SEQ], F32R) for g in range(N_KV)]
            qH = [sb(f"q_hi{b}", [HD + 1, SEQ], F32R) for b in range(Q_RING)]
            qL = [sb(f"q_lo{b}", [HD + 1, SEQ], F32R) for b in range(Q_RING)]
            vv = sb("v_and_ones", [P, NCH, N_KV, P])
            PT = sb("probs", [P, NCH, SEQ])
            sums = sq_sum
        with Arena():
            cH, cL = sb("c_hi", [P, KT, SEQ], F32R), sb("c_lo", [P, KT, SEQ], F32R)
            piece2 = [sb(f"ada2_piece{b}", [P, ADA_W]) for b in range(2)]
            acc2 = sb("ada2_acc", [P, ADA_W])
        with Arena():
            xacc = [sb(f"xb_conv{b}", [P, SEQ]) for b in range(XB)]
            xH = [sb(f"xb_hi{b}", [P, SEQ], F32R) for b in range(XB)]
            xL = [sb(f"xb_lo{b}", [P, SEQ], F32R) for b in range(XB)]
            t2 = sb("tanh_half_log_a", [P, RT, SEQ])
            xbi = sb("gated_x", [P, RT, SEQ])
            yH, yL = xH, xL
        with Arena():
            rope2 = rs_ssd
            ckH, ckL = sb("ckv_hi", [P, CKT, SEQ], F32R), sb("ckv_lo", [P, CKT, SEQ], F32R)
            cqH, cqL = sb("cq_hi", [P, CQT, SEQ], F32R), sb("cq_lo", [P, CQT, SEQ], F32R)
            krH, krL = sb("krope_hi", [QK_ROPE + 1, SEQ], F32R), sb("krope_lo", [QK_ROPE + 1, SEQ], F32R)
            qrH = [sb(f"qrope_hi{b}", [QK_ROPE + 1, SEQ], F32R) for b in range(2)]
            qrL = [sb(f"qrope_lo{b}", [QK_ROPE + 1, SEQ], F32R) for b in range(2)]
            knH, knL, qnH, qnL = ([sb(f"{n}{b}", [P, SEQ], F32R) for b in range(2)]
                                  for n in ("knope_hi", "knope_lo", "qnope_hi", "qnope_lo"))
            vm = [sb(f"v_tok{b}", [P, NCH, V_DIM]) for b in range(2)]
            PT2 = sb("probs2", [P, NCH, SEQ])
            ckf = PT2[:, 0:CQT, :]

        bank = [ctx.enter_context(nc.psum_tensor(f"bank{i}", [P, SEQ], F32)) for i in range(8)]
        PST = bank[2]
        XT, STF, STB, YP = bank[3:7]
        M, S, OP, DEN = bank[3:5], bank[5:7], bank[7], bank[2]
        ADA = bank[7]
        zth = [t[4][:, :], t[5][:, :]]
        t_yz = [xsF[0][:, :], xsF[1][:, :]]

        s_in, s_x, s_rope, s_x2, s_out = sem("inputs_in"), sem("x_in"), sem("rope_in"), sem("x_again"), sem("out_done")
        w_in = [sem(f"slab_in{b}") for b in range(RING)]
        hi_done, lo_done = sem("slab_hi"), sem("slab_lo")
        gemm_done = sem("tile_done")
        evac = [sem(f"tile_evacuated{b}") for b in range(8)]
        v_step, a_step = sem("vector_step"), sem("scalar_step")
        vec_prep = sem("vector_prep")
        ada_in, ada2_in = ([sem(f"{n}{b}") for b in range(w)] for n, w in (("ada_in", ADA_RING), ("ada2_in", 2)))
        ada_acc, ada_red, mod_ready = sem("ada_added"), sem("ada_reduced"), sem("mod_ready")
        c_th = sem("silu_c")
        sq_ready, stat_mm, std_ready, rstd_ready = sem("square"), sem("square_summed"), sem("std"), sem("rstd")
        sq_added = sem("squares_added")
        nfull = sem("normed")
        hiA, hiB, hiC, hiY, hiK, hiX = (sem(f"hi_{n}") for n in "ABCYKX")
        rdyA, rdyB, rdyC, rdyY, rdyK, rdyX = (sem(f"ready_{n}") for n in "ABCYKX")
        sp_x, sp_e = sem("softplus_arg"), sem("softplus_exp")
        a_ready, cs_done, cs_ev, tot_e, cs_sb, cs_dram = (sem(n) for n in ("dt_a", "cs_psum", "cs_tok", "decay_arg",
                                                                           "cs_rows_sb", "cs_rows_dram"))
        wdec, decb = sem("decay_state"), sem("decay_chunk")
        csb_in, e_ready, ed_ready = sem("cs_in"), sem("C_decay"), sem("M_exp")
        conv_th, conv_done, z_th = sem("conv_tanh"), sem("conv_done"), sem("z_tanh")
        xt_done, xs_sc, bt_done, bt_ev, cb_done, cb_ev = (sem(n) for n in ("x_turned", "x_scaled", "B_turned", "B_tok",
                                                                           "CB_psum", "CB_masked"))
        m_ready, ce_ready, st_done, rec_done = sem("M_ready"), sem("CE_ready"), sem("states_psum"), sem("states_run")
        y_done, y_ev, yz_ready = sem("y_psum"), sem("y_out"), sem("y_gated")
        k_ready, q_ready, fills = sem("k_ready"), sem("q_ready"), sem("fills")
        swapped, rot_step, rope_done = sem("halves_swapped"), sem("rotation_product"), sem("roped")
        qk_done, exp_done, pv_done, o_ev = sem("scores"), sem("probs"), sem("pv"), sem("attn_out")
        pair_ready = sem("attn_pair")
        mx_done, mx_red, rows_done, row_ready = sem("max_scores"), sem("max_taken"), sem("max_row"), sem("max_row_in_q")
        mrg = sem("merged")
        lam_e, lam_l = sem("lam_exp"), sem("lam_ln")
        c20, rg_th, ig_th, t2_done, xbi_done, s_done, xbs_done = (sem(n) for n in (
            "conv2_first", "rg_tanh", "ig_tanh", "tanh_half", "gated_x", "sqrt_done", "gated_x_scaled"))
        p_ready, a_exp, am1_done = sem("decay_variance"), sem("decay"), sem("decay_minus_one")
        g_th, y2_ready = sem("gate_tanh"), sem("y2_ready")
        ck_x = sem("c_normed")
        kr_ready, kn_hi, qr_ready, qn_hi, gh_th = (sem(n) for n in (
            "krope", "kn_hi", "qrope", "qn_hi", "gate2_tanh"))
        qk2, exp2, pv2, o2, mxd2, mxr2, rows2, row2, yb = (sem(n) for n in (
            "scores2", "probs2", "pv2", "attn2_out", "max2_scores", "max2_taken", "max2_row", "max2_row_in_q", "attn2_gated"))
        fin_ready = sem("final_ready")
        rope2_in = sem("rope2_in")

        def wait_tile(eng, name):
            eng.wait_ge(gemm_done, TILES[name][0] + 1)

        def wait_evac(eng, name):
            b, used = BANK_OF[name]
            eng.wait_ge(evac[b], used + 1)

        def gb(name):
            return bank[BANK_OF[name][0]]

        def inc_evac(ins, name):
            ins.then_inc(evac[BANK_OF[name][0]], 1)

        def inverses(norm):
            j = NORM_AT[norm]
            return j - (j > NORM_AT["ssd"])

        def r32(ap):
            return ap.bitcast(F32)

        block = ctx.enter_context(nc.Block())

        @block.sync
        def _(sp):
            for n, dst in (("prm", prm), ("cst", cst), ("cstb", cstb), ("tb", tbc)):
                src = d[n].partition_broadcast(P) if n == "tb" else d[n]
                sp.dma_start(dst[:, :], src).then_inc(s_in, 16)
            for p in range(KT):
                if p >= ADA_RING:
                    sp.wait_ge(ada_acc, p - ADA_RING + 1)
                sp.dma_start(piece[p % ADA_RING][:, :], d["ada"][p]).then_inc(ada_in[p % ADA_RING], 16)
                if p == 2:
                    sp.dma_start(xF[:, :, :], d["x"]).then_inc(s_x, 16)
            for s in range(N_SLABS):
                if s >= RING:
                    sp.wait_ge(lo_done, s - RING + 1)
                sp.dma_start(raw[s % RING][:, :], d["ws"][s]).then_inc(w_in[s % RING], 16)
            for m in range(KT):
                sp.wait_ge(fin_ready, m + 1)
                sp.dma_start(d["out"][m], xF[:, m, :]).then_inc(s_out, 16)
            sp.wait_ge(s_out, 16 * KT)

        @block.gpsimd
        def _(pool):
            def fill_attention():
                parts = [(vv[:, :, :, HD:P], 1.0)]
                for g in range(N_KV):
                    parts += [(r32(kH[g][HD:HD + 1, :]), 1.0), (r32(kL[g][HD:HD + 1, :]), 0.0)]
                parts += [(r32(qL[b][HD:HD + 1, :]), 0.0) for b in range(Q_RING)]
                for n, (part, value) in enumerate(parts):
                    nc.gpsimd.memset(part, value).then_inc(fills, 1)
                    pool.wait_ge(fills, n + 1)

            def add_square(norm, k):
                n, step = STAT_AT[norm][0] + k, POOL_AT[norm] + k - 1
                pool.wait_ge(sq_ready, n + 1)
                if k == 1:
                    at = POOLED.index(norm)
                    if at:
                        pool.wait_ge(stat_mm, SUM_AT[POOLED[at - 1]])
                    first = sq[(n - 1) % 2]
                else:
                    pool.wait_ge(sq_added, step)
                    first = sq_sum
                nc.gpsimd.tensor_tensor(sq_sum[:, :], first[:, :], sq[n % 2][:, :], ALU.add).then_inc(sq_added, 1)

            squares = {}
            for i in range(1, PAIRS - 1):
                squares.setdefault(slab_of((between(i + 1) or [("so", N_GROUPS - 1, 0)])[0]) + 2, []).append(("ssd", i))
            for norm, kind in (("n2", "wo"), ("na", "m2"), ("nkv", "oa"), ("fin", "ob")):
                for m in range(1, KT - 1):
                    tile = (kind, FQ - 1, m) if kind == "m2" else (kind, m)
                    squares.setdefault(min((TILES[tile][1] + TILES[tile][2] - 1) // BPS + 3, N_SLABS), []).append((norm, m))

            def rotate(name):
                j = QK_AT[name]
                pool.wait_ge(s_rope, 16)
                pool.wait_ge(swapped, j + 1)
                nc.gpsimd.tensor_tensor(t[3][:, :], t[j % 2][:, :], rope1[:, 0, :], ALU.mult).then_inc(rot_step, 1)
                nc.gpsimd.tensor_tensor(t[2][:, :], t[2][:, :], rope1[:, 1, :], ALU.mult).then_inc(rot_step, 1)
                pool.wait_ge(rot_step, 2 * (j + 1))
                nc.gpsimd.tensor_tensor(t[3][:, :], t[3][:, :], t[2][:, :], ALU.add).then_inc(rope_done, 1)

            turns = {}
            for name in QK:
                turns.setdefault(slab_of(name) + RING + (QK_AT[name] <= KVT), []).append(name)

            for s in range(N_SLABS):
                for name in turns.get(s, ()):
                    rotate(name)
                for norm, k in squares.get(s, ()):
                    add_square(norm, k)
                if s == slab_of(("so", N_GROUPS - 1, KT - 1)):
                    pool.wait_ge(lo_done, s)
                    pool.wait_ge(rdyB, PAIRS)
                    fill_attention()
                pool.wait_ge(hi_done, s + 1)
                nc.gpsimd.tensor_tensor(wlo[s % RING][:, :], raw[s % RING][:, :], r32(whi[s % RING][:, :]),
                                        ALU.subtract).then_inc(lo_done, 1)
            for norm, k in squares.get(N_SLABS, ()):
                add_square(norm, k)

        @block.scalar
        def _(act):
            a = Steps(act, a_step)
            A = nc.scalar.activation
            state = {"hi": 0}

            def hi_upto(s):
                while state["hi"] <= min(s, N_SLABS - 1):
                    n = state["hi"]
                    act.wait_ge(w_in[n % RING], 16 * (n // RING + 1))
                    if n >= RING:
                        act.wait_ge(gemm_done, LAST_TILE.get(n - RING, 0) + 1)
                    A(whi[n % RING][:, :], raw[n % RING][:, :], ACT.Copy).then_inc(hi_done, 1)
                    state["hi"] += 1

            def tile_in(name):
                hi_upto(slab_of(name) + AHEAD)
                wait_tile(act, name)

            def square(norm, k, src, scale=1.0):
                n = STAT_AT[norm][0] + k
                if n >= 2:
                    who, steps = SQ_USED[n - 2]
                    act.wait_ge(stat_mm if who == "pe" else sq_added, steps)
                A(sq[n % 2][:, :], src, ACT.Square, scale=scale).then_inc(sq_ready, 1)

            def root(norm, scale, out=std):
                j = NORM_AT[norm]
                act.wait_ge(stat_mm, SUM_AT[norm])
                if j and out is std:
                    act.wait_ge(rstd_ready, inverses(norm))
                A(out[:, :], PST[:, :], ACT.Sqrt, bias=eps, scale=scale).then_inc(std_ready, 1)

            act.wait_ge(s_in, 64)
            act.wait_ge(vec_prep, 1)
            A(cth, col("c", 0, KT), ACT.Tanh, scale=0.5).then_inc(c_th, 1)
            act.wait_ge(s_x, 16)
            for k in range(KT):
                square("n1", k, xF[:, k, :])
            root("n1", 1.0 / D_MODEL)
            hi_upto(AHEAD)
            for k in range(KT):
                act.wait_ge(nfull, k + 1)
                A(aH[:, k, :], t[k % 2][:, :], ACT.Identity, bias=modc[:, k:k + 1]).then_inc(hiA, 1)

            def conv_act(name):
                q = CONV_AT[name]
                tile_in(name)
                wait_evac(act, name)
                if q >= 2:
                    act.wait_ge(conv_done, q - 1)
                A(t[2 + q % 2][:, :], t[q % 2][:, :], ACT.Tanh).then_inc(conv_th, 1)

            def z_act(i):
                tile_in(("z", i))
                if i >= 2:
                    act.wait_ge(yz_ready, i - 1)
                A(zth[i % 2], gb(("z", i))[:, :], ACT.Tanh, scale=0.5).then_inc(z_th, 1)

            conv_act(("B", 0))
            conv_act(("C", 0))
            tile_in(("dt",))
            act.wait_ge(sp_x, 1)
            A(dtw[:, :, :], dtw[:, :, :], ACT.Exp).then_inc(sp_e, 1)
            A(tbc[:, R2:2 * R2], tbc[:, R2:2 * R2], ACT.Exp).then_inc(sp_e, 1)
            act.wait_ge(lam_e, 1)
            A(lt[:, RT:2 * RT], lt[:, 0:RT], ACT.Exp).then_inc(lam_l, 1)
            conv_act(("xs", 0))
            z_act(0)
            act.wait_ge(cs_done, 1)
            A(csF, YP[0:R2, :], ACT.Copy).then_inc(cs_sb, 1)
            A(decB[:, :, :], STF[:, 0:NCH * R2], ACT.Exp).then_inc(decb, 1)
            act.wait_ge(cs_sb, 1)
            act.dma_start(d["cs"], csF).then_inc(cs_dram, 16)
            act.wait_ge(tot_e, 1)
            A(wS[:, :, :], dtw[:, :, :], ACT.Exp).then_inc(wdec, 1)

            def load_cs(i):
                src = d["cs"].rearrange("(d h) n -> d h n", d=2)[:, 2 * i:2 * i + 2, :]
                act.dma_start(csB[:, :, :].rearrange("p (d h) n -> p d h n", d=2),
                              src.partition_broadcast(P)).then_inc(csb_in, 16)

            act.wait_ge(cs_dram, 16)
            load_cs(0)

            for i in range(PAIRS):
                g = i // PPG
                if i % PPG == 0:
                    act.wait_ge(bt_done, g + 1)
                    A(BT[:, :, :], STB[:, :], ACT.Copy).then_inc(bt_ev, 1)
                act.wait_ge(csb_in, 16 * (i + 1))
                if i:
                    act.wait_ge(y_done, i)
                A(Ex[:, :, :], csB[:, :, :], ACT.Exp).then_inc(e_ready, 1)
                if between(i):
                    hi_upto(slab_of(between(i)[0]) + AHEAD)
                for r in range(4):
                    h = (r // 2) * N_SSD + 2 * i + r % 2
                    for c in range(NCH):
                        w = slice(c * P, (c + 1) * P)
                        a(A(Dm[:, r, w], csB[:, r, w], ACT.Abs, bias=csT[:, c, h:h + 1]))
                    if r % 2:
                        a.settle()
                        A(Dm[:, r - 1:r + 1, :], Dm[:, r - 1:r + 1, :], ACT.Exp, scale=-1.0).then_inc(ed_ready, 1)
                if i + 1 < PAIRS:
                    act.wait_ge(e_ready, i + 1)
                    act.wait_ge(ed_ready, 2 * (i + 1))
                    load_cs(i + 1)
                for name in between(i):
                    if name[0] == "z":
                        z_act(i + 1)
                    elif name[0] == "so":
                        hi_upto(slab_of(name) + AHEAD)
                    else:
                        conv_act(name)
                act.wait_ge(yz_ready, i + 1)
                A(bH[:, i % KT, :], t_yz[i % 2], ACT.Copy, scale=w05[:, i:i + 1]).then_inc(hiB, 1)
                square("ssd", i, t_yz[i % 2], 0.5)
            hi_upto(slab_of(("so", N_GROUPS - 1, KT - 1)) + AHEAD)
            root("ssd", 1.0 / D_INNER, rs_ssd)

            act.wait_ge(y_done, PAIRS)
            act.wait_ge(ce_ready, PAIRS)
            act.dma_start(rope1[:, :, :], d["rope1"]).then_inc(s_rope, 16)

            def qk_copy(name):
                j = QK_AT[name]
                tile_in(name)
                square(name, 0, gb(name)[:, :])
                if j >= 2:
                    act.wait_ge(rope_done, j - 1)
                inc_evac(A(t[j % 2][:, :], gb(name)[:, :], ACT.Copy, scale=col(name[0] + "n")), name)

            def qk_norm(name):
                qk_copy(name)
                root(name, 1.0)

            for name in QK[:KVT + 1]:
                qk_norm(name)
            for c in range(NCH):
                tile_in(("v", c))
                inc_evac(A(vv[:, c, :, 0:HD], gb(("v", c))[:, 0:N_KV * HD].rearrange("p (g d) -> p g d", g=N_KV),
                           ACT.Copy), ("v", c))
            qk_norm(QK[KVT + 1])

            def max_row(h):
                act.wait_ge(rows_done, h + 1)
                A(qH[h % Q_RING][HD:HD + 1, :], M[0][0:1, :], ACT.Copy, scale=-1.0).then_inc(row_ready, 1)

            def round_pair(u):
                act.wait_ge(pair_ready, u + 1)
                if u == 0:
                    wait_tile(act, ("so", N_GROUPS - 1, KT - 1))
                A(bH[:, u, :], t[4 + u % 2][:, :], ACT.Copy).then_inc(hiB, 1)

            max_row(0)
            for h in range(N_Q):
                u = h // 2
                for c in range(NCH):
                    n = NCH * h + c
                    act.wait_ge(qk_done, n + 1)
                    if h:
                        act.wait_ge(pv_done, n - NCH + 1)
                    A(PT[:, c, :], S[n % 2][:, :], ACT.Exp, scale=HD ** -0.5).then_inc(exp_done, 1)
                if h % 2 == 0 and u:
                    round_pair(u - 1)
                if h % 2 == 0 and u + 2 < QT:
                    qk_copy(("q", u + 2))
                if h + 1 < N_Q:
                    max_row(h + 1)
                if h % 2 == 0 and u + 2 < QT:
                    root(("q", u + 2), 1.0)
            round_pair(QT - 1)

            def ada2_load(p):
                if p >= KT + 2:
                    act.wait_ge(ada_acc, p - 1)
                act.dma_start(piece2[p % 2][:, :], d["ada"][p]).then_inc(ada2_in[p % 2], 16)

            act.wait_ge(pv_done, NCH * N_Q)
            act.wait_ge(rope_done, KVT + QT)
            ada2_load(KT)
            ada2_load(KT + 1)
            for m in range(KT):
                tile_in(("ga", m))
                if m >= 2:
                    act.wait_ge(mrg, m - 1)
                inc_evac(A(t[m % 2][:, :], gb(("ga", m))[:, :], ACT.Tanh, scale=0.5), ("ga", m))
                tile_in(("gs", m))
                inc_evac(A(t[2 + m % 2][:, :], gb(("gs", m))[:, :], ACT.Tanh, scale=0.5), ("gs", m))
                hi_upto(slab_of(("wa", m)) + AHEAD)
                act.wait_ge(mrg, m + 1)
                A(cH[:, m, :], t[4 + m % 2][:, :], ACT.Copy, scale=0.5).then_inc(hiC, 1)
                for p in (KT + 2 * m + 2, KT + 2 * m + 3):
                    if p < ADA_G * KT:
                        ada2_load(p)
            act.dma_start(xF[:, :, :], d["x"]).then_inc(s_x2, 16)
            for m in range(KT):
                hi_upto(slab_of(("wo", m)) + AHEAD)
                wait_evac(act, ("wo", m))
                square("n2", m, xF[:, m, :])
            root("n2", 1.0 / D_MODEL)
            for k in range(KT):
                act.wait_ge(nfull, KT + k + 1)
                A(aH[:, k, :], t[k % 2][:, :], ACT.Identity, bias=modc[:, 3 * KT + k:3 * KT + k + 1]).then_inc(hiA, 1)

            for f in range(FQ):
                for m in range(KT):
                    n = KT * f + m
                    tile_in(("m1", f, m))
                    if n >= 2:
                        act.wait_ge(rdyB, 24 + n - 1)
                    inc_evac(A(t[2 + n % 2][:, :], gb(("m1", f, m))[:, :], ACT.Relu), ("m1", f, m))
                    wait_evac(act, ("m1", f, m))
                    A(bH[:, m, :], t[2 + n % 2][:, :], ACT.Square).then_inc(hiB, 1)
                for m in range(KT):
                    hi_upto(slab_of(("m2", f, m)) + AHEAD)
                    if f == FQ - 1:
                        wait_evac(act, ("m2", f, m))
                        square("na", m, xF[:, m, :])

            root("na", 1.0 / D_MODEL)
            for k in range(KT):
                act.wait_ge(nfull, 2 * KT + k + 1)
                A(aH[:, k, :], t[k % 2][:, :], ACT.Copy).then_inc(hiA, 1)

            def gates(n):
                tile_in(("rg", n))
                if n >= 1:
                    act.wait_ge(a_exp, n)
                else:
                    act.wait_ge(hiB, 24 + KT * FQ)
                inc_evac(A(t[2][:, :], gb(("rg", n))[:, :], ACT.Tanh, scale=0.5, bias=hbr[:, n:n + 1]), ("rg", n))
                tile_in(("ig", n))
                if n >= 2:
                    act.wait_ge(xbi_done, n - 1)
                inc_evac(A(t[4 + n % 2][:, :], gb(("ig", n))[:, :], ACT.Tanh, scale=0.5,
                           bias=hbr[:, RT + n:RT + n + 1]), ("ig", n))
                wait_evac(act, ("rg", n))
                A(t2[:, n, :], t[2][:, :], ACT.Tanh, scale=nsp[:, n:n + 1], bias=nsp[:, n:n + 1]).then_inc(t2_done, 1)
                if n:
                    act.wait_ge(am1_done, n)
                A(t[3][:, :], t[2][:, :], ACT.Exp, scale=nsp2[:, n:n + 1], bias=nsp2[:, n:n + 1]).then_inc(a_exp, 1)

            act.wait_ge(lam_e, 2)
            for n in range(RT):
                tile_in(("xb", n))
                if n >= XB:
                    act.wait_ge(xbi_done, n - XB + 1)
                A(xacc[n % XB][:, :], gb(("xb", n))[:, :], ACT.Identity, scale=col("cw2", 3 * RT + n),
                  bias=col("cb2", n)).then_inc(c20, 1)
                wait_evac(act, ("xb", n))
                if n >= XB:
                    wait_tile(act, ("ig", n - XB))
                A(xH[n % XB][:, :], xacc[n % XB][:, :], ACT.Copy).then_inc(hiX, 1)
                if n >= RNN_LAG:
                    gates(n - RNN_LAG)
            for n in range(RT - RNN_LAG, RT):
                gates(n)
            hi_upto(slab_of(("gt", 0)) + 1)
            act.wait_ge(am1_done, RT)
            for n in range(RT):
                if n >= 2:
                    act.wait_ge(xbs_done, n - 1)
                act.wait_ge(p_ready, n + 1)
                A(t[2 + n % 2][:, :], t[n % 2][:, :], ACT.Sqrt, scale=-0.25).then_inc(s_done, 1)
                hi_upto(slab_of(("gt", n // 2)) + AHEAD)
            for n in range(RT):
                hi_upto(slab_of(("gt", min(n + 2, RT - 1))) + AHEAD)
                tile_in(("gt", n))
                A(t[4 + n % 2][:, :], gb(("gt", n))[:, :], ACT.Tanh, scale=0.5).then_inc(g_th, 1)
                act.wait_ge(y2_ready, n + 1)
                dst, ev = (bH[:, n, :], hiB) if n < KT else (yH[n - KT][:, :], hiY)
                A(dst, t[n % 2][:, :], ACT.Copy, scale=0.5).then_inc(ev, 1)
            for m in range(KT):
                hi_upto(slab_of(("oa", m)) + AHEAD)
                wait_evac(act, ("oa", m))
                square("nkv", m, xF[:, m, :])

            act.wait_ge(xbs_done, RT)
            act.wait_ge(rdyY, RT - KT)
            act.dma_start(rope2[:, :], d["rope2"]).then_inc(rope2_in, 16)
            root("nkv", 1.0 / D_MODEL)
            for k in range(KT):
                act.wait_ge(nfull, 3 * KT + k + 1)
                A(aH[:, k, :], t[k % 2][:, :], ACT.Copy).then_inc(hiA, 1)
            for i in range(CKT):
                tile_in(("ck", i))
                square("ckv", i, gb(("ck", i))[:, :])
                inc_evac(A(ckf[:, i, :], gb(("ck", i))[:, :], ACT.Copy), ("ck", i))
            hi_upto(slab_of(("kr",)) + AHEAD)
            for k in range(KT):
                act.wait_ge(nfull, 4 * KT + k + 1)
                A(bH[:, k, :], t[k % 2][:, :], ACT.Copy).then_inc(hiB, 1)
            hi_upto(slab_of(("cq", 0)) + AHEAD)
            root("ckv", 1.0 / KV_RANK)
            hi_upto(slab_of(("cq", 1)) + AHEAD)
            for i in range(CKT):
                act.wait_ge(ck_x, i + 1)
                A(ckH[:, i, :], t[i % 2][:, :], ACT.Copy).then_inc(hiK, 1)
            hi_upto(slab_of(("kr",)) + AHEAD)
            for i in range(CQT):
                tile_in(("cq", i))
                square("cq", i, gb(("cq", i))[:, :])
                if i < CKT:
                    act.wait_ge(ck_x, i + 1)
                inc_evac(A(ckf[:, i, :], gb(("cq", i))[:, :], ACT.Copy), ("cq", i))
            root("cq", 1.0 / Q_RANK)
            for i in range(CQT):
                act.wait_ge(ck_x, CKT + i + 1)
                A(cqH[:, i, :], t[i % 2][:, :], ACT.Copy).then_inc(hiK, 1)

            def head_gemms1(h):
                hi_upto(slab_of(("qn", h)) + AHEAD)
                tile_in(("kn", h))
                A(knH[h % 2][:, :], gb(("kn", h))[:, :], ACT.Copy).then_inc(kn_hi, 1)
                tile_in(("qn", h))
                A(qnH[h % 2][:, :], gb(("qn", h))[:, :], ACT.Copy).then_inc(qn_hi, 1)

            def max_row2(h):
                act.wait_ge(rows2, h + 1)
                A(qrH[h % 2][QK_ROPE:QK_ROPE + 1, :], M[0][0:1, :], ACT.Copy, scale=-1.0).then_inc(row2, 1)

            def head_gemms2(h):
                tile_in(("vh", h))
                inc_evac(A(vm[h % 2][:, :, :], gb(("vh", h))[:, :], ACT.Copy), ("vh", h))
                hi_upto(slab_of(("gh", h)) + AHEAD)
                max_row2(h)
                tile_in(("gh", h))
                A(t[4 + h % 2][:, :], gb(("gh", h))[:, :], ACT.Tanh, scale=0.5).then_inc(gh_th, 1)

            head_gemms1(0)
            head_gemms2(0)
            for h in range(N_HEADS):
                for c in range(NCH):
                    n = NCH * h + c
                    act.wait_ge(qk2, n + 1)
                    if h:
                        act.wait_ge(pv2, n - NCH + 1)
                    A(PT2[:, c, c * P:SEQ], S[n % 2][:, c * P:SEQ], ACT.Exp,
                      scale=(QK_NOPE + QK_ROPE) ** -0.5).then_inc(exp2, 1)
                if h + 1 < N_HEADS:
                    head_gemms1(h + 1)
                    head_gemms2(h + 1)
                act.wait_ge(yb, h + 1)
                A(aH[:, h, :], t[2][:, :], ACT.Copy, scale=0.5).then_inc(hiA, 1)
            for m in range(KT):
                hi_upto(slab_of(("ob", m)) + AHEAD)
                wait_evac(act, ("ob", m))
                square("fin", m, xF[:, m, :])
            root("fin", 1.0 / D_MODEL)

        @block.tensor
        def _(pe):
            mm = nc.tensor.matmul

            def start(name):
                b, used = BANK_OF[name]
                if used:
                    pe.wait_ge(evac[b], used)

            def weights(name):
                _, at, blocks = TILES[name]
                for n in range(at, at + blocks):
                    if n == at or n % BPS == 0:
                        pe.wait_ge(lo_done, n // BPS + 1)
                    yield n // BPS % RING, (n % BPS) * P

            def split_mm(out, lh, ll, rh, rl, first, last):
                mm(out, lh, rh, start=first, stop=False)
                mm(out, lh, rl, start=False, stop=False)
                return mm(out, ll, rh, start=False, stop=last)

            def feature_tile(name, hi, lo, ready=None):
                start(name)
                blocks = TILES[name][2]
                for k, (b, o) in enumerate(weights(name)):
                    if ready:
                        pe.wait_ge(ready[0], ready[1] + k + 1)
                    ins = split_mm(gb(name)[:, :], whi[b][:, o:o + P], wlo[b][:, o:o + P], hi(k), lo(k), k == 0,
                                   k == blocks - 1)
                ins.then_inc(gemm_done, 1)

            def in_a(k):
                return aH[:, k, :]

            def in_a_lo(k):
                return aL[:, k, :]

            def in_b(k):
                return bH[:, k, :]

            def in_b_lo(k):
                return bL[:, k, :]

            def stat(norm, k, ones_=None):
                j, (n0, w) = NORM_AT[norm], STAT_AT[norm]
                n = n0 + k
                if norm in POOLED and k < w - 1:
                    return
                pe.wait_ge(sq_ready, n + 1)
                if j and (k == 0 or norm in POOLED):
                    pe.wait_ge(std_ready, j)
                o = ones if ones_ is None else ones_
                if norm in POOLED:
                    pe.wait_ge(sq_added, POOL_AT[norm] + w - 2)
                    mm(PST[:, :], o, sq_sum[:, :], start=True, stop=False)
                mm(PST[:, :], o, sq[n % 2][:, :], start=(k == 0), stop=(k == w - 1)).then_inc(stat_mm, 1)

            def ada_reduce(src, j):
                pe.wait_ge(ada_acc, KT * (j + 1))
                if j:
                    pe.wait_ge(mod_ready, j)
                for b in range(ADA_W // P):
                    ins = mm(ADA[:, b:b + 1], src[:, b * P:(b + 1) * P], ones[:, 0:1], start=True, stop=True)
                ins.then_inc(ada_red, 1)

            pe.wait_ge(s_in, 64)
            for k in range(KT):
                stat("n1", k)
            ada_reduce(acc, 0)

            for n in (("B", 0), ("C", 0)):
                feature_tile(n, in_a, in_a_lo, (rdyA, 0))
            name = ("dt",)
            start(name)
            blk = list(weights(name))
            for c in range(NCH):
                for k in range(KT):
                    b, o = blk[k // 2]
                    o += k % 2 * R2
                    ins = split_mm(gb(name)[:, c * R2:(c + 1) * R2], aH[:, k, c * P:(c + 1) * P],
                                   aL[:, k, c * P:(c + 1) * P], whi[b][:, o:o + R2], wlo[b][:, o:o + R2], k == 0,
                                   k == KT - 1)
            ins.then_inc(gemm_done, 1)
            feature_tile(("xs", 0), in_a, in_a_lo)
            feature_tile(("z", 0), in_a, in_a_lo)
            pe.wait_ge(a_ready, 1)
            for c in range(NCH):
                for dd, tri in ((0, trif), (1, trib)):
                    r = slice(dd * N_SSD, (dd + 1) * N_SSD)
                    mm(STB[:, c * R2 + dd * N_SSD:c * R2 + (dd + 1) * N_SSD], tri, aT[:, c, r], start=True, stop=True)
                    mm(YP[r, c * P:(c + 1) * P], aT[:, c, r], tri, start=True, stop=True)
                ins = mm(STF[:, c * R2:(c + 1) * R2], ones, aT[:, c, :], start=True, stop=True)
            ins.then_inc(cs_done, 1)
            pe.wait_ge(decb, 1)
            pe.wait_ge(tot_e, 1)

            def mixer_tile(name):
                if name[0] != "so":
                    feature_tile(name, in_a, in_a_lo)
                    return
                half = name[1] % 2 * PPG
                feature_tile(name, lambda k: bH[:, half + k, :], lambda k: bL[:, half + k, :], (rdyB, PPG * name[1]))

            for i in range(PAIRS):
                g, pg = i // PPG, i % PPG
                pe.wait_ge(conv_done, CONV_AT[("xs", i)] + 1)
                if i:
                    pe.wait_ge(xs_sc, i)
                for c in range(NCH):
                    ins = nc.tensor.transpose(XT[:, c * P:(c + 1) * P], xsF[i % 2][:, c * P:(c + 1) * P], ident)
                ins.then_inc(xt_done, 1)
                if pg == 0:
                    pe.wait_ge(conv_done, CONV_AT[("C", g)] + 1)
                    if g:
                        pe.wait_ge(bt_ev, g)
                        pe.wait_ge(rec_done, i)
                    for c in range(NCH):
                        ins = nc.tensor.transpose(STB[:, c * P:(c + 1) * P], BF[g % 2][:, c * P:(c + 1) * P], ident)
                    ins.then_inc(bt_done, 1)
                    for c in range(NCH):
                        w = slice(c * P, (c + 1) * P)
                        ins = mm(STF[:, w], BF[g % 2][:, w], CF[g % 2][:, w], start=True, stop=True)
                    ins.then_inc(cb_done, 1)
                names = between(i)
                if i + 1 < PAIRS:
                    mixer_tile(names.pop(0))
                if i:
                    stat("ssd", i - 1)
                pe.wait_ge(xs_sc, i + 1)
                pe.wait_ge(bt_ev, g + 1)
                pe.wait_ge(cb_ev, 2 * (g + 1))
                if i:
                    pe.wait_ge(rec_done, i)
                for c in range(NCH - 1):
                    mm(STF[:, c * P:(c + 1) * P], BT[:, c, :], XS[0][:, c, :], start=True, stop=True)
                    ins = mm(STB[:, c * P:(c + 1) * P], BT[:, c + 1, :], XS[1][:, c + 1, :], start=True, stop=True)
                ins.then_inc(st_done, 1)
                for name in names:
                    mixer_tile(name)
                pe.wait_ge(m_ready, 2 * (i + 1))
                pe.wait_ge(ce_ready, i + 1)
                pe.wait_ge(rec_done, i + 1)
                if i:
                    pe.wait_ge(y_ev, i)
                halves = [slice(hh * HD, (hh + 1) * HD) for hh in range(2)]
                for c in range(NCH):
                    w = slice(c * P, (c + 1) * P)
                    for hh, hp in enumerate(halves):
                        mm(YP[hp, w], XS[2][:, c, hp], Dm[:, hh, w], start=True, stop=False)
                    if c:
                        for hh, hp in enumerate(halves):
                            mm(YP[hp, w], prev[:, 0, c - 1, hp], Ex[:, hh, w], start=False, stop=False)
                    if c < NCH - 1:
                        for hh, hp in enumerate(halves):
                            mm(YP[hp, w], prev[:, 1, c, hp], Ex[:, 2 + hh, w], start=False, stop=False)
                    for hh, hp in enumerate(halves):
                        ins = mm(YP[hp, w], XS[3][:, c, hp], Dm[:, 2 + hh, w], start=False, stop=True)
                ins.then_inc(y_done, 1)
            stat("ssd", PAIRS - 1)
            for m in range(KT):
                mixer_tile(("so", N_GROUPS - 1, m))

            for n, name in enumerate(QK[:KVT + 1]):
                feature_tile(name, in_a, in_a_lo)
                if n:
                    stat(QK[n - 1], 0, blk64)
            stat(QK[KVT], 0, blk64)
            W2 = KVT * P
            blk = list(weights(("v", 0)))
            for c in range(NCH):
                start(("v", c))
                for k in range(KT):
                    b, o = blk[KVT * k]
                    ins = split_mm(gb(("v", c))[:, 0:W2], aH[:, k, c * P:(c + 1) * P], aL[:, k, c * P:(c + 1) * P],
                                   whi[b][:, o:o + W2], wlo[b][:, o:o + W2], k == 0, k == KT - 1)
                ins.then_inc(gemm_done, 1)
            feature_tile(QK[KVT + 1], in_a, in_a_lo)

            def scores_for_max(h, i):
                n = NCH * h + i
                if i == 0:
                    pe.wait_ge(q_ready, h + 1)
                    pe.wait_ge(k_ready, h // 4 + 1)
                    if h:
                        pe.wait_ge(row_ready, h)
                if n >= 2:
                    pe.wait_ge(mx_red, n - 1)
                mm(M[i % 2][:, :], qH[h % Q_RING][0:HD, i * P:(i + 1) * P], kH[h // 4][0:HD, :], start=True,
                   stop=True).then_inc(mx_done, 1)

            def row_of_max(h):
                pe.wait_ge(mx_red, NCH * (h + 1))
                for i in range(NCH):
                    ins = nc.tensor.transpose(M[0][0:1, i * P:(i + 1) * P], mx[h % 2][:, i:i + 1], ident)
                ins.then_inc(rows_done, 1)

            def scores(h, c):
                g, b = h // 4, h % Q_RING
                if c == 0:
                    pe.wait_ge(row_ready, h + 1)
                    pe.wait_ge(fills, 1 + 2 * N_KV + Q_RING)
                n = NCH * h + c
                w = slice(c * P, (c + 1) * P)
                if n >= 2:
                    pe.wait_ge(exp_done, n - 1)
                split_mm(S[n % 2][:, :], kH[g][:, w], kL[g][:, w], qH[b][:, :], qL[b][:, :], True,
                         True).then_inc(qk_done, 1)

            def values(h, c):
                pe.wait_ge(exp_done, NCH * h + c + 1)
                if c == 0 and h:
                    pe.wait_ge(o_ev, h)
                mm(OP[:, :], vv[:, c, h // 4, :], PT[:, c, :], start=(c == 0), stop=(c == NCH - 1)).then_inc(pv_done, 1)

            pe.wait_ge(y_ev, PAIRS)
            for i in range(NCH):
                scores_for_max(0, i)
            row_of_max(0)
            stat(QK[KVT + 1], 0, blk64)
            for c in range(NCH):
                wait_evac(pe, ("v", c))
            for h in range(N_Q):
                u = h // 2
                for c in range(NCH):
                    scores(h, c)
                    if h + 1 < N_Q:
                        scores_for_max(h + 1, c)
                if h % 2 == 0 and u + 2 < QT:
                    feature_tile(("q", u + 2), in_a, in_a_lo)
                for c in range(NCH):
                    values(h, c)
                    if c == 0 and h + 1 < N_Q:
                        row_of_max(h + 1)
                    if c == 1 and h % 2 == 0 and u + 2 < QT:
                        stat(("q", u + 2), 0, blk64)

            for m in range(KT):
                feature_tile(("ga", m), in_a, in_a_lo)
                feature_tile(("gs", m), in_a, in_a_lo)
                feature_tile(("wa", m), in_b, in_b_lo, (rdyB, PAIRS))
                if m == KT // 2:
                    pe.wait_ge(o_ev, N_Q)
                    ada_reduce(acc2, 1)
            for m in range(KT):
                feature_tile(("wo", m), lambda k: cH[:, k, :], lambda k: cL[:, k, :], (rdyC, 0))
                if m == KT // 2:
                    ada_reduce(acc2, 2)
                if m:
                    stat("n2", m - 1)
            stat("n2", KT - 1)

            for f in range(FQ):
                for m in range(KT):
                    feature_tile(("m1", f, m), in_a, in_a_lo, (rdyA, KT))
                for m in range(KT):
                    feature_tile(("m2", f, m), in_b, in_b_lo, (rdyB, 24 + KT * f))
                    if f == FQ - 1 and m:
                        stat("na", m - 1)
            stat("na", KT - 1)

            def gates(n):
                for w in ("rg", "ig"):
                    feature_tile((w, n), lambda k: xH[n % XB][:, :], lambda k: xL[n % XB][:, :], (rdyX, n))

            for n in range(RT):
                feature_tile(("xb", n), in_a, in_a_lo, (rdyA, 2 * KT))
                if n >= RNN_LAG:
                    gates(n - RNN_LAG)
            for n in range(RT - RNN_LAG, RT):
                gates(n)
            for n in range(RT):
                feature_tile(("gt", n), in_a, in_a_lo)
            pe.wait_ge(rdyB, 24 + KT * FQ + KT)
            pe.wait_ge(rdyY, RT - KT)
            for m in range(KT):
                feature_tile(("oa", m), lambda k: bH[:, k, :] if k < KT else yH[k - KT][:, :],
                             lambda k: bL[:, k, :] if k < KT else yL[k - KT][:, :])
                if m:
                    stat("nkv", m - 1)
            stat("nkv", KT - 1)

            for i in range(CKT):
                feature_tile(("ck", i), in_a, in_a_lo, (rdyA, 3 * KT))
            feature_tile(("kr",), in_a, in_a_lo)
            for i in range(CKT):
                stat("ckv", i)
            for i in range(CQT):
                feature_tile(("cq", i), in_b, in_b_lo, (rdyB, 24 + KT * FQ + KT))
                if i:
                    stat("cq", i - 1)
            stat("cq", CQT - 1)

            def head_gemms1(h):
                feature_tile(("qr", h), lambda k: cqH[:, k, :], lambda k: cqL[:, k, :], (rdyK, CKT))
                feature_tile(("kn", h), lambda k: ckH[:, k, :], lambda k: ckL[:, k, :], (rdyK, 0))
                feature_tile(("qn", h), lambda k: cqH[:, k, :], lambda k: cqL[:, k, :])

            def head_values(h):
                name = ("vh", h)
                start(name)
                blk = list(weights(name))
                for c in range(NCH):
                    w = slice(c * P, (c + 1) * P)
                    for k, (b, o) in enumerate(blk):
                        ins = split_mm(gb(name)[:, w], ckH[:, k, w], ckL[:, k, w], whi[b][:, o:o + P],
                                       wlo[b][:, o:o + P], k == 0, k == CKT - 1)
                ins.then_inc(gemm_done, 1)

            def scores_for_max2(h, i):
                n = NCH * h + i
                b = h % 2
                if i == 0:
                    pe.wait_ge(kr_ready, 1)
                    wait_evac(pe, ("kn", h))
                    pe.wait_ge(qr_ready, h + 1)
                    wait_evac(pe, ("qn", h))
                    if h:
                        pe.wait_ge(row2, h)
                if n >= 2:
                    pe.wait_ge(mxr2, n - 1)
                w, keys = slice(i * P, (i + 1) * P), (i + 1) * P
                out = M[i % 2][:, 0:keys]
                mm(out, qnH[b][:, w], knH[b][:, 0:keys], start=True, stop=False)
                mm(out, qrH[b][0:QK_ROPE, w], krH[0:QK_ROPE, 0:keys], start=False, stop=False)
                mm(M[i % 2][:, w], identb, mask_qk, start=False, stop=True).then_inc(mxd2, 1)

            def row_of_max2(h):
                pe.wait_ge(mxr2, NCH * (h + 1))
                for i in range(NCH):
                    ins = nc.tensor.transpose(M[0][0:1, i * P:(i + 1) * P], mx[h % 2][:, i:i + 1], ident)
                ins.then_inc(rows2, 1)

            def scores2(h):
                b = h % 2
                pe.wait_ge(row2, h + 1)
                for c in range(NCH):
                    n = NCH * h + c
                    w, q = slice(c * P, (c + 1) * P), slice(c * P, SEQ)
                    if n >= 2:
                        pe.wait_ge(exp2, n - 1)
                    out = S[n % 2][:, q]
                    split_mm(out, knH[b][:, w], knL[b][:, w], qnH[b][:, q], qnL[b][:, q], True, False)
                    split_mm(out, krH[:, w], krL[:, w], qrH[b][:, q], qrL[b][:, q], False, False)
                    mm(S[n % 2][:, w], identb, mask_kq, start=False, stop=True).then_inc(qk2, 1)

            def values2(h, c):
                pe.wait_ge(exp2, NCH * h + c + 1)
                if c == 0 and h:
                    pe.wait_ge(o2, h)
                q = slice(c * P, SEQ)
                mm(OP[:, q], vm[h % 2][:, c, :], PT2[:, c, q], start=(c == 0), stop=(c == NCH - 1))
                mm(DEN[:, q], ones, PT2[:, c, q], start=(c == 0), stop=(c == NCH - 1)).then_inc(pv2, 1)

            head_gemms1(0)
            head_values(0)
            for i in range(NCH):
                scores_for_max2(0, i)
            row_of_max2(0)
            feature_tile(("gh", 0), in_b, in_b_lo)
            for h in range(N_HEADS):
                scores2(h)
                if h + 1 < N_HEADS:
                    head_gemms1(h + 1)
                    head_values(h + 1)
                    for i in range(NCH):
                        scores_for_max2(h + 1, i)
                wait_evac(pe, ("vh", h))
                for c in range(NCH):
                    values2(h, c)
                if h + 1 < N_HEADS:
                    row_of_max2(h + 1)
                    feature_tile(("gh", h + 1), in_b, in_b_lo)
            for m in range(KT):
                feature_tile(("ob", m), in_a, in_a_lo, (rdyA, 4 * KT))
                if m:
                    stat("fin", m - 1)
            stat("fin", KT - 1)

        @block.vector
        def _(ve):
            v = Steps(ve, v_step)
            V = nc.vector

            ve.wait_ge(s_in, 64)
            v(V.memset(eps, EPS))
            v(V.tensor_scalar(cwh, prm[:, PCOL["cw"][0]:PCOL["cw"][0] + 6 * 24], 0.5, None, ALU.mult))
            v(V.tensor_scalar(w05, col("ssdn", 0, PAIRS), 0.5, None, ALU.mult))
            V.tensor_scalar(hbr, prm[:, PCOL["brg"][0]:PCOL["brg"][0] + 2 * RT], 0.5, None, ALU.mult).then_inc(vec_prep, 1)
            V.scalar_tensor_tensor(lt[:, 0:RT], col("lam", 0, RT), -1.0, col("lam", 0, RT), ALU.mult, ALU.min)\
                .then_inc(lam_e, 1)
            ve.wait_ge(c_th, 1)
            v(V.tensor_scalar(csl, cth, 0.5, 0.5, ALU.mult, ALU.add))
            v.settle()
            v(V.tensor_tensor(csl, csl, col("c", 0, KT), ALU.mult))
            v.settle()

            def ada_add(p, into):
                k = p % KT
                if p < KT:
                    src = piece[p % ADA_RING]
                    ve.wait_ge(ada_in[p % ADA_RING], 16 * (p // ADA_RING + 1))
                else:
                    src = piece2[p % 2]
                    ve.wait_ge(ada2_in[p % 2], 16 * ((p - KT) // 2 + 1))
                if k == 0:
                    if p:
                        ve.wait_ge(ada_red, p // KT)
                    V.tensor_scalar(into[:, :], src[:, :], csl[:, 0:1], None, ALU.mult).then_inc(ada_acc, 1)
                else:
                    ve.wait_ge(ada_acc, p)
                    V.scalar_tensor_tensor(into[:, :], src[:, :], csl[:, k:k + 1], into[:, :], ALU.mult,
                                           ALU.add).then_inc(ada_acc, 1)

            def ada_finish(j):
                ve.wait_ge(ada_red, j + 1)
                w = slice(2 * KT * j, 2 * KT * (j + 1))
                V.tensor_tensor(modc[:, w], ADA[:, 0:2 * KT], col("bada", 2 * KT * j, 2 * KT), ALU.add)\
                    .then_inc(mod_ready, 1)
                ve.wait_ge(mod_ready, j + 1)

            def inverse(norm):
                ve.wait_ge(std_ready, NORM_AT[norm] + 1)
                V.reciprocal(rstd[:, :], std[:, :]).then_inc(rstd_ready, 1)
                ve.wait_ge(rstd_ready, inverses(norm) + 1)

            def norm_split(n0, gain, hi, lo, hi_sem, hi0, rdy, shift=None):
                def low(k):
                    ve.wait_ge(hi_sem, hi0 + k + 1)
                    if shift is None:
                        ins = V.tensor_tensor(lo[:, k, :], t[k % 2][:, :], r32(hi[:, k, :]), ALU.subtract)
                    else:
                        ins = V.scalar_tensor_tensor(lo[:, k, :], t[k % 2][:, :], shift(k), r32(hi[:, k, :]), ALU.add,
                                                     ALU.subtract)
                    ins.then_inc(rdy, 1)

                for k in range(KT):
                    if k >= 2:
                        low(k - 2)
                        ve.wait_ge(rdy, hi0 + k - 1)
                    V.scalar_tensor_tensor(t[k % 2][:, :], xF[:, k, :], gain(k), rstd[:, :], ALU.mult, ALU.mult)\
                        .then_inc(nfull, 1)
                low(KT - 2)
                low(KT - 1)
                ve.wait_ge(rdy, hi0 + KT)

            for p in range(KT - 1):
                ada_add(p, acc)
            inverse("n1")
            ada_add(KT - 1, acc)
            ada_finish(0)
            v(V.scalar_tensor_tensor(gain1, modc[:, KT:2 * KT], 1.0, col("norm1", 0, KT), ALU.add, ALU.mult))
            v.settle()
            norm_split(0, lambda k: gain1[:, k:k + 1], aH, aL, hiA, 0, rdyA, lambda k: modc[:, k:k + 1])

            def log1p(e, z, z2, p):
                v(V.tensor_scalar(p, e, 2.0, None, ALU.add))
                v.settle()
                v(V.reciprocal(p, p))
                v.settle()
                v(V.scalar_tensor_tensor(z, e, 2.0, p, ALU.mult, ALU.mult))
                v.settle()
                v(V.scalar_tensor_tensor(z2, z, 0.25, z, ALU.mult, ALU.mult))
                v.settle()
                v(V.tensor_scalar(p, z2, 1.0 / (2 * LOG_TERMS + 1), None, ALU.mult))
                v.settle()
                for k in range(LOG_TERMS - 1, 0, -1):
                    v(V.scalar_tensor_tensor(p, p, 1.0 / (2 * k + 1), z2, ALU.add, ALU.mult))
                    v.settle()
                v(V.scalar_tensor_tensor(p, p, 1.0, z, ALU.add, ALU.mult))
                v.settle()

            def conv_taps(name):
                q = CONV_AT[name]
                i = {"xs": name[1], "B": 16 + name[1], "C": 20 + name[1]}[name[0]]
                out, src = t[q % 2], gb(name)
                wait_tile(ve, name)
                v(V.tensor_scalar(out[:, :], src[:, :], cwh[:, 2 * 24 + i:2 * 24 + i + 1],
                                  cwh[:, 5 * 24 + i:5 * 24 + i + 1], ALU.mult, ALU.add))
                v.settle()
                for n, j in enumerate((0, 1, 3, 4)):
                    sh = j - 2
                    o = slice(max(0, -sh), SEQ - max(0, sh))
                    s = slice(max(0, sh), SEQ + min(0, sh))
                    ins = V.scalar_tensor_tensor(out[:, o], src[:, s], cwh[:, j * 24 + i:j * 24 + i + 1], out[:, o],
                                                 ALU.mult, ALU.add)
                    if n < 3:
                        v(ins)
                        v.settle()
                    else:
                        inc_evac(ins, name)

            def conv_silu(name):
                q = CONV_AT[name]
                out = t[q % 2]
                dst = {"xs": xsF, "B": BF, "C": CF}[name[0]][name[1] % 2]
                ve.wait_ge(conv_th, q + 1)
                V.scalar_tensor_tensor(dst[:, :], t[2 + q % 2][:, :], 1.0, out[:, :], ALU.add, ALU.mult)\
                    .then_inc(conv_done, 1)

            def z_gate(i):
                name = ("z", i)
                ve.wait_ge(z_th, i + 1)
                inc_evac(V.scalar_tensor_tensor(zth[i % 2], zth[i % 2], 1.0, gb(name)[:, :], ALU.add, ALU.mult), name)

            for name in (("B", 0), ("C", 0)):
                conv_taps(name)
                conv_silu(name)
            name = ("dt",)
            wait_tile(ve, name)
            psum = gb(name)[:, 0:NCH * R2].rearrange("p (c r) -> p c r", c=NCH)
            bias = tbc[:, None, 0:R2].broadcast_to([P, NCH, R2])
            inc_evac(V.tensor_tensor(dtT[:, :, :], psum, bias, ALU.add), name)
            wait_evac(ve, name)
            V.scalar_tensor_tensor(dtw[:, :, :], dtT[:, :, :], -1.0, dtT[:, :, :], ALU.mult, ALU.min).then_inc(sp_x, 1)
            ve.wait_ge(sp_e, 1)
            log1p(dtw[:, :, :], decB[:, :, :], dtx[:, :, :], wS[:, :, :])
            v(V.scalar_tensor_tensor(dtT[:, :, :], dtT[:, :, :], 0.0, wS[:, :, :], ALU.max, ALU.add))
            v.settle()
            ve.wait_ge(sp_e, 2)
            V.scalar_tensor_tensor(aT[:, :, :], dtT[:, :, :], -1.0, tbc[:, None, R2:2 * R2].broadcast_to([P, NCH, R2]),
                                   ALU.mult, ALU.mult).then_inc(a_ready, 1)
            ve.wait_ge(lam_l, 1)
            e, lp = lt[:, RT:2 * RT], lt[:, 2 * RT:3 * RT]
            log1p(e, lt[:, 3 * RT:4 * RT], lt[:, 0:RT], lp)
            v(V.scalar_tensor_tensor(e, col("lam", 0, RT), 0.0, lp, ALU.min, ALU.subtract))
            v.settle()
            v(V.tensor_scalar(nsp2, e, 4.0, None, ALU.mult))
            V.tensor_scalar(nsp, e, 2.0, None, ALU.mult).then_inc(lam_e, 1)

            conv_taps(("xs", 0))
            conv_silu(("xs", 0))
            z_gate(0)
            ve.wait_ge(cs_done, 1)
            v(V.tensor_scalar(csT[:, :, :], STB[:, 0:NCH * R2], -1.0, None, ALU.mult))
            v.settle()
            ve.wait_ge(decb, 1)
            V.tensor_tensor(dtw[:, :, :], STF[:, 0:NCH * R2].rearrange("p (c r) -> p c r", c=NCH), csT[:, :, :],
                            ALU.add).then_inc(tot_e, 1)
            ve.wait_ge(wdec, 1)
            v(V.tensor_tensor(wS[:, :, :], wS[:, :, :], dtT[:, :, :], ALU.mult))
            v.settle()

            def so_evac(name):
                _, g, m = name
                wait_tile(ve, name)
                if g == 0:
                    inc_evac(V.tensor_copy(xF[:, m, :], gb(name)[:, :]), name)
                else:
                    inc_evac(V.tensor_tensor(xF[:, m, :], xF[:, m, :], gb(name)[:, :], ALU.add), name)

            def gated_low(i):
                ve.wait_ge(hiB, i + 1)
                ve.wait_ge(yz_ready, i + 1)
                V.scalar_tensor_tensor(bL[:, i % KT, :], t_yz[i % 2], w05[:, i:i + 1], r32(bH[:, i % KT, :]), ALU.mult,
                                       ALU.subtract).then_inc(rdyB, 1)

            for i in range(PAIRS):
                g, pg = i // PPG, i % PPG
                ve.wait_ge(xt_done, i + 1)
                if i:
                    ve.wait_ge(y_done, i)
                xt = XT[:, :].rearrange("p (c h d) -> p c h d", c=NCH, h=2)
                for n, (buf, tab, dd) in enumerate(((XS[0], wS, 0), (XS[1], wS, 1), (XS[2], dtT, 0), (XS[3], dtT, 1))):
                    h0 = dd * N_SSD + 2 * i
                    ins = V.tensor_tensor(buf[:, :, :].rearrange("p c (h d) -> p c h d", h=2), xt,
                                          tab[:, :, h0:h0 + 2, None].broadcast_to([P, NCH, 2, HD]), ALU.mult)
                ins.then_inc(xs_sc, 1)
                if i:
                    gated_low(i - 1)
                if pg == 0:
                    ve.wait_ge(cb_done, g + 1)
                    for buf, tri in zip(CB, (trif, trib)):
                        V.tensor_tensor(buf[:, :].rearrange("p (c l) -> p c l", c=NCH),
                                        STF[:, :].rearrange("p (c l) -> p c l", c=NCH),
                                        tri[:, None, :].broadcast_to([P, NCH, P]), ALU.mult).then_inc(cb_ev, 1)
                ve.wait_ge(e_ready, i + 1)
                V.tensor_tensor(Ex[:, :, :], Ex[:, :, :], CF[g % 2][:, None, :].broadcast_to([P, 4, SEQ]), ALU.mult)\
                    .then_inc(ce_ready, 1)
                names = between(i)
                if i + 1 < PAIRS:
                    conv_taps(names.pop(0))
                ve.wait_ge(st_done, i + 1)
                v(V.tensor_copy(prev[:, 0, 0, :], STF[:, 0:P]))
                v(V.tensor_copy(prev[:, 1, 2, :], STB[:, 2 * P:3 * P]))
                for n in (1, 2):
                    v.settle()
                    for dd, slot, src in ((0, n, n - 1), (1, 2 - n, 3 - n)):
                        ps = (STF, STB)[dd]
                        c = n if dd == 0 else 3 - n
                        for hh in range(2):
                            hp = slice(hh * HD, (hh + 1) * HD)
                            h = dd * N_SSD + 2 * i + hh
                            st = ps[:, (c if dd == 0 else c - 1) * P + hh * HD:(c if dd == 0 else c - 1) * P + (hh + 1) * HD]
                            ins = V.scalar_tensor_tensor(prev[:, dd, slot, hp], prev[:, dd, src, hp],
                                                         decB[:, c, h:h + 1], st, ALU.mult, ALU.add)
                            if n == 2 and dd == 1 and hh == 1:
                                ins.then_inc(rec_done, 1)
                            else:
                                v(ins)
                for name in names:
                    if name[0] in ("B", "C"):
                        conv_taps(name)
                ve.wait_ge(cb_ev, 2 * (g + 1))
                for dd in range(2):
                    ve.wait_ge(ed_ready, 2 * i + dd + 1)
                    V.tensor_tensor(Dm[:, 2 * dd:2 * dd + 2, :], Dm[:, 2 * dd:2 * dd + 2, :],
                                    CB[dd][:, None, :].broadcast_to([P, 2, SEQ]), ALU.mult).then_inc(m_ready, 1)
                for name in names:
                    if name[0] == "so":
                        so_evac(name)
                for name in between(i):
                    if name[0] in ("xs", "B", "C"):
                        conv_silu(name)
                if i + 1 < PAIRS:
                    z_gate(i + 1)
                ve.wait_ge(y_done, i + 1)
                wait_evac(ve, ("z", i))
                yz = t_yz[i % 2]
                V.scalar_tensor_tensor(yz, yz, col("ssdD", i), YP[:, :], ALU.mult, ALU.add).then_inc(y_ev, 1)
                ve.wait_ge(y_ev, i + 1)
                V.tensor_tensor(yz, yz, zth[i % 2], ALU.mult).then_inc(yz_ready, 1)
            gated_low(PAIRS - 1)
            for m in range(KT):
                so_evac(("so", N_GROUPS - 1, m))

            def rotate(name):
                j = QK_AT[name]
                wait_evac(ve, name)
                V.stream_shuffle(t[2][:, :], t[j % 2][:, :], SWAP).then_inc(swapped, 1)
                inverse(name)

            def split_heads(name, outs, ready, before):
                ve.wait_ge(rope_done, QK_AT[name] + 1)
                for hh, (hi, lo) in enumerate(outs):
                    hp = slice(hh * HD, (hh + 1) * HD)
                    v(V.tensor_tensor(t[2][0:HD, :], t[3][hp, :], rstd[hp, :], ALU.mult))
                    v.settle()
                    v(V.tensor_copy(hi[0:HD, :], t[2][0:HD, :]))
                    v.settle()
                    V.tensor_tensor(lo[0:HD, :], t[2][0:HD, :], r32(hi[0:HD, :]), ALU.subtract).then_inc(ready, 1)
                    ve.wait_ge(ready, before + hh + 1)

            def turn_k(j):
                rotate(("k", j))
                split_heads(("k", j), [(kH[2 * j], kL[2 * j]), (kH[2 * j + 1], kL[2 * j + 1])], k_ready, 2 * j)

            def split_q(u):
                b = 2 * u % Q_RING
                if u > 2:
                    ve.wait_ge(qk_done, NCH * 2 * (u - 2))
                split_heads(("q", u), [(qH[b], qL[b]), (qH[b + 1], qL[b + 1])], q_ready, 2 * u)

            def share_pair(u):
                ve.wait_ge(o_ev, 2 * (u + 1))
                v.settle()
                v(V.reciprocal(sums[:, :], sums[:, :]))
                v.settle()
                V.tensor_tensor(t[4 + u % 2][:, :], t[4 + u % 2][:, :], sums[:, :], ALU.mult).then_inc(pair_ready, 1)
                ve.wait_ge(pair_ready, u + 1)

            def split_pair(u):
                ve.wait_ge(hiB, PAIRS + u + 1)
                V.tensor_tensor(bL[:, u, :], t[4 + u % 2][:, :], r32(bH[:, u, :]), ALU.subtract).then_inc(rdyB, 1)
                ve.wait_ge(rdyB, PAIRS + u + 1)

            def max_of(h, i):
                ve.wait_ge(mx_done, NCH * h + i + 1)
                if i == 0 and h >= 2:
                    ve.wait_ge(rows_done, h - 1)
                V.tensor_reduce(mx[h % 2][:, i:i + 1], M[i % 2][:, :], AX, ALU.max).then_inc(mx_red, 1)

            turn_k(0)
            rotate(("q", 0))
            split_q(0)
            turn_k(1)
            for i in range(NCH):
                max_of(0, i)
            rotate(("q", 1))
            split_q(1)
            for h in range(N_Q):
                u = h // 2
                if h + 1 < N_Q:
                    for i in range(NCH):
                        max_of(h + 1, i)
                if h % 2 == 0 and u:
                    share_pair(u - 1)
                    split_pair(u - 1)
                    if u + 1 < QT:
                        split_q(u + 1)
                if h % 2 and u + 2 < QT:
                    rotate(("q", u + 2))
                ve.wait_ge(pv_done, NCH * (h + 1))
                hp, at = slice(h % 2 * HD, (h % 2 + 1) * HD), t[4 + u % 2]
                v(V.tensor_copy(sums[hp, :], OP[HD:P, :]))
                V.tensor_copy(at[hp, :], OP[0:HD, :]).then_inc(o_ev, 1)
            share_pair(QT - 1)
            split_pair(QT - 1)

            v(V.reciprocal(rs_ssd[:, :], rs_ssd[:, :]))
            v.settle()

            for m in range(KT):
                out = t[4 + m % 2]
                wait_evac(ve, ("gs", m))
                v(V.scalar_tensor_tensor(xF[:, m, :], t[2 + m % 2][:, :], 1.0, xF[:, m, :], ALU.add, ALU.mult))
                v.settle()
                v(V.tensor_tensor(xF[:, m, :], xF[:, m, :], rs_ssd[:, :], ALU.mult))
                if m >= 2:
                    ve.wait_ge(hiC, m - 1)
                wait_tile(ve, ("wa", m))
                wait_evac(ve, ("ga", m))
                inc_evac(V.scalar_tensor_tensor(out[:, :], t[m % 2][:, :], 1.0, gb(("wa", m))[:, :], ALU.add, ALU.mult),
                         ("wa", m))
                wait_evac(ve, ("wa", m))
                v.settle()
                V.tensor_tensor(out[:, :], out[:, :], xF[:, m, :], ALU.add).then_inc(mrg, 1)
                ve.wait_ge(hiC, m + 1)
                ve.wait_ge(mrg, m + 1)
                V.scalar_tensor_tensor(cL[:, m, :], out[:, :], 0.5, r32(cH[:, m, :]), ALU.mult, ALU.subtract)\
                    .then_inc(rdyC, 1)
                if m == KT // 2:
                    ada_finish(1)
                for p in (KT + 2 * m, KT + 2 * m + 1):
                    ada_add(p, acc2)
            ve.wait_ge(s_x2, 16)
            for m in range(KT):
                name = ("wo", m)
                wait_tile(ve, name)
                inc_evac(V.scalar_tensor_tensor(xF[:, m, :], gb(name)[:, :], modc[:, 2 * KT + m:2 * KT + m + 1],
                                                xF[:, m, :], ALU.mult, ALU.add), name)
                if m == KT // 2:
                    ada_finish(2)
                    v(V.scalar_tensor_tensor(gain2, modc[:, 4 * KT:5 * KT], 1.0, col("norm2", 0, KT), ALU.add, ALU.mult))
            v.settle()
            inverse("n2")
            norm_split(KT, lambda k: gain2[:, k:k + 1], aH, aL, hiA, KT, rdyA,
                       lambda k: modc[:, 3 * KT + k:3 * KT + k + 1])

            for f in range(FQ):
                for m in range(KT):
                    n = KT * f + m
                    wait_evac(ve, ("m1", f, m))
                    r, full = t[2 + n % 2], t[4 + n % 2]
                    v(V.tensor_tensor(full[:, :], r[:, :], r[:, :], ALU.mult))
                    v.settle()
                    ve.wait_ge(hiB, 24 + n + 1)
                    V.tensor_tensor(bL[:, m, :], full[:, :], r32(bH[:, m, :]), ALU.subtract).then_inc(rdyB, 1)
                for m in range(KT):
                    name = ("m2", f, m)
                    wait_tile(ve, name)
                    inc_evac(V.scalar_tensor_tensor(xF[:, m, :], gb(name)[:, :], modc[:, 5 * KT + m:5 * KT + m + 1],
                                                    xF[:, m, :], ALU.mult, ALU.add), name)

            inverse("na")
            norm_split(2 * KT, lambda k: col("na", k), aH, aL, hiA, 2 * KT, rdyA)

            def scale_x(n):
                ve.wait_ge(s_done, n + 1)
                V.tensor_tensor(xbi[:, n, :], xbi[:, n, :], t[n % 2 + 2][:, :], ALU.mult).then_inc(xbs_done, 1)

            def conv_rnn(n):
                name, out = ("xb", n), xacc[n % XB]
                ve.wait_ge(c20, n + 1)
                for j in range(3):
                    sh = 3 - j
                    ins = V.scalar_tensor_tensor(out[:, sh:SEQ], gb(name)[:, 0:SEQ - sh], col("cw2", j * RT + n),
                                                 out[:, sh:SEQ], ALU.mult, ALU.add)
                    if j < 2:
                        v(ins)
                        v.settle()
                    else:
                        inc_evac(ins, name)
                ve.wait_ge(hiX, n + 1)
                wait_evac(ve, name)
                V.tensor_tensor(xL[n % XB][:, :], out[:, :], r32(xH[n % XB][:, :]), ALU.subtract).then_inc(rdyX, 1)

            def gate_x(n):
                wait_evac(ve, ("ig", n))
                V.scalar_tensor_tensor(xbi[:, n, :], t[4 + n % 2][:, :], 1.0, xacc[n % XB][:, :], ALU.add, ALU.mult)\
                    .then_inc(xbi_done, 1)

            def decay(n):
                ve.wait_ge(a_exp, n + 1)
                V.scalar_tensor_tensor(t2[:, n, :], t[3][:, :], 1.0, t2[:, n, :], ALU.add, ALU.mult).then_inc(am1_done, 1)

            for n in range(RT):
                conv_rnn(n)
                if n >= RNN_LAG:
                    gate_x(n - RNN_LAG)
                    decay(n - RNN_LAG)
            for n in range(RT - RNN_LAG, RT):
                gate_x(n)
                decay(n)
            ve.wait_ge(xbi_done, RT)
            ve.wait_ge(am1_done, RT)
            for n in range(RT):
                if n >= 2:
                    ve.wait_ge(s_done, n - 1)
                V.scalar_tensor_tensor(t[n % 2][:, :], t2[:, n, :], 2.0, t2[:, n, :], ALU.add, ALU.mult)\
                    .then_inc(p_ready, 1)
                if n:
                    scale_x(n - 1)
            scale_x(RT - 1)
            ve.wait_ge(xbs_done, RT)
            for n in range(RT):
                name, th = ("gt", n), t[4 + n % 2]
                v(V.tensor_scalar(t2[:, n, :], t2[:, n, :], 1.0, None, ALU.add))
                v.settle()
                v(V.tensor_tensor_scan(xacc[1][:, :], t2[:, n, :], xbi[:, n, :], 0.0, ALU.mult, ALU.add))
                ve.wait_ge(g_th, n + 1)
                inc_evac(V.scalar_tensor_tensor(th[:, :], th[:, :], 1.0, gb(name)[:, :], ALU.add, ALU.mult), name)
                wait_evac(ve, name)
                v.settle()
                V.tensor_tensor(t[n % 2][:, :], xacc[1][:, :], th[:, :], ALU.mult).then_inc(y2_ready, 1)
                if n < KT:
                    ve.wait_ge(hiB, 24 + KT * FQ + n + 1)
                    hi, lo, rdy, r0 = bH[:, n, :], bL[:, n, :], rdyB, 24 + KT * FQ + n
                else:
                    ve.wait_ge(hiY, n - KT + 1)
                    hi, lo, rdy, r0 = yH[n - KT][:, :], yL[n - KT][:, :], rdyY, n - KT
                V.scalar_tensor_tensor(lo, t[n % 2][:, :], 0.5, r32(hi), ALU.mult, ALU.subtract).then_inc(rdy, 1)
                ve.wait_ge(rdy, r0 + 1)

            def add_to_stream(name, m):
                wait_tile(ve, name)
                inc_evac(V.tensor_tensor(xF[:, m, :], xF[:, m, :], gb(name)[:, :], ALU.add), name)

            for m in range(KT):
                add_to_stream(("oa", m), m)

            inverse("nkv")
            norm_split(3 * KT, lambda k: col("nkv", k), aH, aL, hiA, 3 * KT, rdyA)
            norm_split(4 * KT, lambda k: col("nb", k), bH, bL, hiB, 24 + KT * FQ + KT, rdyB)

            v(V.memset(r32(krH[QK_ROPE:QK_ROPE + 1, :]), 1.0))
            v(V.memset(r32(krL[QK_ROPE:QK_ROPE + 1, :]), 0.0))
            for b in range(2):
                v(V.memset(r32(qrL[b][QK_ROPE:QK_ROPE + 1, :]), 0.0))

            def compress(norm, gain, n0, tiles, lo):
                def low(i):
                    ve.wait_ge(hiK, n0 + i + 1)
                    hi = (ckH if lo is ckL else cqH)[:, i, :]
                    V.tensor_tensor(lo[:, i, :], t[i % 2][:, :], r32(hi), ALU.subtract).then_inc(rdyK, 1)

                inverse(norm)
                for i in range(tiles):
                    if i >= 2:
                        low(i - 2)
                        ve.wait_ge(rdyK, n0 + i - 1)
                    V.scalar_tensor_tensor(t[i % 2][:, :], ckf[:, i, :], col(gain, i), rstd[:, :], ALU.mult, ALU.mult)\
                        .then_inc(ck_x, 1)
                for i in range(max(0, tiles - 2), tiles):
                    low(i)

            def rope(name, hi, lo, ready):
                wait_tile(ve, name)
                R = QK_ROPE
                v(V.tensor_tensor(t[0][0:R, :], gb(name)[0:R, :], rope2[0:R, :], ALU.mult))
                inc_evac(V.tensor_tensor(t[1][0:R, :], gb(name)[R:P, :], rope2[R:P, :], ALU.mult), name)
                wait_evac(ve, name)
                v.settle()
                v(V.tensor_tensor(t[0][0:R, :], t[0][0:R, :], t[1][0:R, :], ALU.add))
                v.settle()
                v(V.tensor_copy(hi[0:R, :], t[0][0:R, :]))
                v.settle()
                V.tensor_tensor(lo[0:R, :], t[0][0:R, :], r32(hi[0:R, :]), ALU.subtract).then_inc(ready, 1)

            compress("ckv", "kvn", 0, CKT, ckL)
            ve.wait_ge(rope2_in, 16)
            ve.wait_ge(rdyK, CKT)
            rope(("kr",), krH, krL, kr_ready)
            compress("cq", "qn2", CKT, CQT, cqL)

            def head_low(h):
                b = h % 2
                rope(("qr", h), qrH[b], qrL[b], qr_ready)
                for n, hi, lo, done in (("kn", knH, knL, kn_hi), ("qn", qnH, qnL, qn_hi)):
                    ve.wait_ge(done, h + 1)
                    inc_evac(V.tensor_tensor(lo[b][:, :], gb((n, h))[:, :], r32(hi[b][:, :]), ALU.subtract), (n, h))

            def max2_of(h):
                for i in range(NCH):
                    ve.wait_ge(mxd2, NCH * h + i + 1)
                    if i == 0 and h >= 2:
                        ve.wait_ge(rows2, h - 1)
                    V.tensor_reduce(mx[h % 2][:, i:i + 1], M[i % 2][:, 0:(i + 1) * P], AX, ALU.max).then_inc(mxr2, 1)

            def gate2(h):
                ve.wait_ge(gh_th, h + 1)
                inc_evac(V.scalar_tensor_tensor(t[4 + h % 2][:, :], t[4 + h % 2][:, :], 1.0, gb(("gh", h))[:, :], ALU.add,
                                                ALU.mult), ("gh", h))

            head_low(0)
            max2_of(0)
            gate2(0)
            for h in range(N_HEADS):
                if h + 1 < N_HEADS:
                    head_low(h + 1)
                    max2_of(h + 1)
                ve.wait_ge(pv2, NCH * (h + 1))
                v(V.reciprocal(t[3][:, :], DEN[:, :]))
                v.settle()
                V.tensor_tensor(t[3][:, :], OP[:, :], t[3][:, :], ALU.mult).then_inc(o2, 1)
                ve.wait_ge(o2, h + 1)
                wait_evac(ve, ("gh", h))
                V.tensor_tensor(t[2][:, :], t[3][:, :], t[4 + h % 2][:, :], ALU.mult).then_inc(yb, 1)
                if h + 1 < N_HEADS:
                    gate2(h + 1)
                ve.wait_ge(hiA, 4 * KT + h + 1)
                ve.wait_ge(yb, h + 1)
                V.scalar_tensor_tensor(aL[:, h, :], t[2][:, :], 0.5, r32(aH[:, h, :]), ALU.mult, ALU.subtract)\
                    .then_inc(rdyA, 1)
            for m in range(KT):
                add_to_stream(("ob", m), m)
            inverse("fin")
            for m in range(KT):
                V.scalar_tensor_tensor(xF[:, m, :], xF[:, m, :], col("fin", m), rstd[:, :], ALU.mult, ALU.mult)\
                    .then_inc(fin_ready, 1)


def kernel(x, c, w_ada, b_ada, norm1_w, norm2_w, w_in, q_norm_w, k_norm_w, conv_w, conv_b, A_log, dt_bias, ssd_D,
           ssd_norm_w, w_attn_out, w_ssd_out, w_o, w_mlp1, w_mlp2, norm_a_2, w_in_a_2, conv_w_2, conv_b_2, w_rg_2,
           b_rg_2, w_ig_2, b_ig_2, lru_lambda_2, w_out_a_2, norm_kv_2, w_dkv_2, kv_norm_2, w_uk_2, w_uv_2, norm_b_2,
           w_in_b_2, q_norm_2, w_uq_2, w_out_b_2, final_norm_2):
    import ml_dtypes
    import numpy as np
    import concourse.bacc as bacc
    from concourse.bass_utils import run_bass_kernel_spmd

    f32 = np.float32

    def arr(a):
        return np.asarray(a, f32)

    w_in, w_in_b, w_in_a = arr(w_in)[0], arr(w_in_b_2)[0], arr(w_in_a_2)[0]
    w_so, w_wa, w_wo = arr(w_ssd_out)[0], arr(w_attn_out)[0], arr(w_o)[0]
    w_m1, w_m2, w_oa, w_ob = arr(w_mlp1)[0], arr(w_mlp2)[0], arr(w_out_a_2)[0], arr(w_out_b_2)[0]
    w_rg, w_ig, w_dkv = arr(w_rg_2)[0], arr(w_ig_2)[0], arr(w_dkv_2)
    w_uk, w_uv, w_uq = arr(w_uk_2), arr(w_uv_2), arr(w_uq_2)[0]
    HR = QK_ROPE // 2

    o_k = N_Q * HD
    o_v = o_k + N_KV * HD
    o_xs = o_v + N_KV * HD
    o_B = o_xs + D_INNER
    o_C = o_B + N_GROUPS * D_STATE
    o_z = o_C + N_GROUPS * D_STATE
    o_dt = o_z + D_INNER
    o_ga = o_dt + 2 * N_SSD
    o_gs = o_ga + D_MODEL

    def cols(w, a, i=0, n=P):
        return w[:, a + n * i:a + n * (i + 1)]

    def with_swapped_halves(w):
        return np.concatenate([w, w[:, HR:], w[:, :HR]], axis=1)

    def matrix(name):
        kind, i = name[0], name[1] if len(name) > 1 else 0
        return {
            "dt": lambda: cols(w_in, o_dt, 0, 2 * N_SSD), "B": lambda: cols(w_in, o_B, i),
            "C": lambda: cols(w_in, o_C, i), "xs": lambda: cols(w_in, o_xs, i), "z": lambda: cols(w_in, o_z, i),
            "so": lambda: cols(w_so[PPG * P * i:PPG * P * (i + 1)], 0, name[2]),
            "k": lambda: cols(w_in, o_k, i), "v": lambda: cols(w_in, o_v, 0, N_KV * HD), "q": lambda: cols(w_in, 0, i),
            "ga": lambda: cols(w_in, o_ga, i), "gs": lambda: cols(w_in, o_gs, i), "wa": lambda: cols(w_wa, 0, i),
            "wo": lambda: cols(w_wo, 0, i), "m1": lambda: cols(w_m1, D_MODEL * i, name[2]),
            "m2": lambda: cols(w_m2[D_MODEL * i:D_MODEL * (i + 1)], 0, name[2]),
            "xb": lambda: cols(w_in_a, 0, i), "gt": lambda: cols(w_in_a, D_RNN, i), "rg": lambda: w_rg[i],
            "ig": lambda: w_ig[i], "oa": lambda: cols(w_oa, 0, i), "ck": lambda: cols(w_dkv, 0, i),
            "kr": lambda: with_swapped_halves(w_dkv[:, KV_RANK:]), "cq": lambda: cols(w_in_b, 0, i),
            "qr": lambda: with_swapped_halves(w_uq[:, i, QK_NOPE:]), "kn": lambda: w_uk[:, i],
            "qn": lambda: w_uq[:, i, :QK_NOPE], "vh": lambda: w_uv[:, i], "gh": lambda: cols(w_in_b, Q_RANK, i),
            "ob": lambda: cols(w_ob, 0, i)}[kind]()

    stream = np.zeros((P, N_SLABS * SLAB), f32)
    at = 0
    for name, blocks in ORDER:
        if name != "pad":
            w = matrix(name)
            stream[:, at:at + blocks * P] = w.reshape(-1, P, w.shape[1]).transpose(1, 0, 2).reshape(P, -1)
        at += blocks * P
    stream = np.ascontiguousarray(stream.reshape(P, N_SLABS, SLAB).transpose(1, 0, 2))

    def feat(a):
        return arr(a).reshape(-1, P).T

    vectors = {
        "norm1": feat(norm1_w), "norm2": feat(norm2_w), "qn": feat(np.tile(arr(q_norm_w).ravel(), P // HD)),
        "kn": feat(np.tile(arr(k_norm_w).ravel(), P // HD)), "cw": feat(conv_w), "cb": feat(conv_b),
        "ssdD": feat(np.repeat(arr(ssd_D).ravel(), HD)), "ssdn": feat(ssd_norm_w), "na": feat(norm_a_2),
        "cw2": feat(conv_w_2), "cb2": feat(conv_b_2), "brg": feat(b_rg_2), "big": feat(b_ig_2),
        "lam": feat(lru_lambda_2), "nkv": feat(norm_kv_2), "kvn": feat(kv_norm_2), "nb": feat(norm_b_2),
        "qn2": feat(q_norm_2), "fin": feat(final_norm_2), "bada": feat(b_ada), "c": feat(c)}
    prm = np.ascontiguousarray(np.concatenate([vectors[n] for n, _ in _PRM], axis=1))

    r, s = np.arange(P)[:, None], np.arange(P)[None, :]
    blk = (r // HD == s // HD) / HD
    cst = np.concatenate([r == s, r <= s, r >= s, np.ones((P, P)), blk], axis=1).astype(f32)
    cstb = np.concatenate([r == s, np.where(s >= r, 0.0, -1e30), np.where(s <= r, 0.0, -1e30)], axis=1)
    cstb = cstb.astype(ml_dtypes.bfloat16)
    tok = np.arange(SEQ, dtype=f32)
    dim = np.arange(P) % HD
    half = HD // 2
    freq = 10000.0 ** (-2.0 * (dim % half % (half // 2)) / half)
    pos = np.where((dim < half)[:, None], tok[None] // 64, tok[None] % 64)
    ang = (pos.astype(f32) * freq[:, None].astype(f32)).astype(np.float64)
    sign = np.where(dim % half < half // 2, -1.0, 1.0)[:, None]
    rope1 = np.ascontiguousarray(np.stack([np.cos(ang), sign * np.sin(ang)], axis=1).astype(f32))
    dim = np.arange(QK_ROPE)
    freq = 10000.0 ** (-2.0 * (dim % HR) / QK_ROPE)
    ang = (tok[None] * freq[:, None].astype(f32)).astype(f32).astype(np.float64)
    sign = np.where(dim < HR, -1.0, 1.0)[:, None]
    rope2 = np.concatenate([np.cos(ang), sign * np.sin(ang)], axis=0).astype(f32)

    inputs = {
        "prm": prm, "cst": cst, "cstb": cstb, "ws": stream, "rope1": rope1, "rope2": rope2,
        "tb": np.ascontiguousarray(np.concatenate([arr(dt_bias).ravel(), arr(A_log).ravel()])),
        "ada": np.ascontiguousarray(arr(w_ada)[0].reshape(KT, P, ADA_G, ADA_W).transpose(2, 0, 1, 3)
                                    .reshape(ADA_G * KT, P, ADA_W)),
        "x": np.ascontiguousarray(arr(x)[0].T.reshape(KT, P, SEQ).transpose(1, 0, 2))}

    nc = bacc.Bacc("TRN2", target_bir_lowering=False, num_devices=1)
    d = {n: nc.dram_tensor(n, a.shape, BF16 if a.dtype != f32 else F32, kind="ExternalInput").ap()
         for n, a in inputs.items()}
    d["cs"] = nc.dram_tensor("cs_scratch", (2 * N_SSD, SEQ), F32, kind="Internal").ap()
    d["out"] = nc.dram_tensor("out", (KT, P, SEQ), F32, kind="ExternalOutput").ap()
    build(nc, d)
    res = run_bass_kernel_spmd(nc, [inputs], core_ids=[0])
    out = np.asarray(res.results[0]["out"]).reshape(D_MODEL, SEQ)
    return np.ascontiguousarray(out.T)[None]
```
